# Optimizing a Trainium2 kernel written in Bass

```python
import jax, jax.numpy as jnp
from jax import lax
import numpy as np

D_MODEL = 2048
BATCH = 1
SEQ = 256
DEPTH = 1

BRANCH_W = D_MODEL // 2
N_BRANCH = 3
RW_HEAD = 64
RW_HEADS = BRANCH_W // RW_HEAD
RW_DECAY_RANK = 64
RW_AAA_RANK = 64
RW_LN_EPS = 64e-5
RW_COLS = 4 * BRANCH_W + RW_DECAY_RANK + RW_AAA_RANK
SSD_HEAD = 64
SSD_HEADS = BRANCH_W // SSD_HEAD
SSD_GROUPS = 4
SSD_STATE = 128
SSD_CONV = 4
SSD_CHUNK = 128
SSD_XBC = BRANCH_W + 2 * SSD_GROUPS * SSD_STATE
SSD_COLS = BRANCH_W + SSD_XBC + SSD_HEADS
SSD_NORM_EPS = 1e-5
SC_CONV = 3
SC_COLS = 4 * BRANCH_W
GATE_COLS = N_BRANCH * D_MODEL
IN_COLS = RW_COLS + SSD_COLS + SC_COLS + GATE_COLS
NORM_EPS = 1e-6

kernel_name = "hybrid_rwkv7_mamba2_shortconv_gated_merge"

def rmsnorm(x, w, eps=NORM_EPS):
    x32 = x.astype(jnp.float32)
    y = x32 * lax.rsqrt(jnp.mean(x32 * x32, axis=-1, keepdims=True) + eps)
    return (y * w.astype(jnp.float32)).astype(x.dtype)

def causal_dwconv(x, w):
    k_width, ch = w.shape
    return lax.conv_general_dilated(
        x, w[:, None, :].astype(x.dtype), window_strides=(1,),
        padding=[(k_width - 1, 0)], dimension_numbers=('NWC', 'WIO', 'NWC'),
        feature_group_count=ch)

def token_shift(p, mu):
    prev = jnp.pad(p, ((0, 0), (1, 0), (0, 0)))[:, :-1]
    return p + mu * (prev - p)

def rwkv7_branch(pa, mu, w0, w2, a0, a2, k_k, k_a, r_k, ln_w, ln_b):
    bsz, seq, _ = pa.shape
    pa = token_shift(pa.astype(jnp.float32), mu)
    r, k, v, g, dw, da = jnp.split(
        pa, [BRANCH_W, 2 * BRANCH_W, 3 * BRANCH_W, 4 * BRANCH_W, 4 * BRANCH_W + RW_DECAY_RANK], axis=-1)
    log_w = -jax.nn.softplus(-(w0 + jnp.tanh(dw) @ w2)) - 0.5
    decay = jnp.exp(-jnp.exp(log_w))
    a = jax.nn.sigmoid(a0 + da @ a2)
    kk = k * k_k
    k = k * (1.0 + (a - 1.0) * k_a)
    heads = lambda t: t.reshape(bsz, seq, RW_HEADS, RW_HEAD)
    r, k, v, kk, a, decay = (heads(t) for t in (r, k, v, kk, a, decay))
    kh = kk / jnp.maximum(jnp.sqrt(jnp.sum(kk * kk, axis=-1, keepdims=True)), 1e-12)
    bvec = kh * a

    def step(s, inp):
        r_t, w_t, k_t, v_t, kh_t, b_t = inp
        sa = jnp.einsum('bhvk,bhk->bhv', s, kh_t)
        s = s * w_t[:, :, None, :] - sa[..., None] * b_t[:, :, None, :] + v_t[..., None] * k_t[:, :, None, :]
        return s, jnp.einsum('bhvk,bhk->bhv', s, r_t)

    tm = lambda t: jnp.moveaxis(t, 1, 0)
    s0 = jnp.zeros((bsz, RW_HEADS, RW_HEAD, RW_HEAD), jnp.float32)
    _, y = lax.scan(step, s0, (tm(r), tm(decay), tm(k), tm(v), tm(kh), tm(bvec)))
    y = jnp.moveaxis(y, 0, 1)
    mean = jnp.mean(y, axis=-1, keepdims=True)
    var = jnp.mean(jnp.square(y - mean), axis=-1, keepdims=True)
    yn = (y - mean) * lax.rsqrt(var + RW_LN_EPS)
    yn = yn * ln_w.reshape(RW_HEADS, RW_HEAD) + ln_b.reshape(RW_HEADS, RW_HEAD)
    bonus = jnp.sum(r * k * r_k, axis=-1, keepdims=True) * v
    return (yn + bonus).reshape(bsz, seq, BRANCH_W) * jax.nn.silu(g)

def ssd_chunked(xdt, da, bm, cm):
    bsz, seq, n_heads, hd = xdt.shape
    n_chunks = seq // SSD_CHUNK
    hpg = n_heads // SSD_GROUPS
    xc = xdt.reshape(bsz, n_chunks, SSD_CHUNK, SSD_GROUPS, hpg, hd)
    bc = bm.reshape(bsz, n_chunks, SSD_CHUNK, SSD_GROUPS, SSD_STATE)
    cc = cm.reshape(bsz, n_chunks, SSD_CHUNK, SSD_GROUPS, SSD_STATE)
    a_cs = jnp.cumsum(da.reshape(bsz, n_chunks, SSD_CHUNK, SSD_GROUPS, hpg).transpose(0, 1, 3, 4, 2), axis=-1)
    causal = jnp.tril(jnp.ones((SSD_CHUNK, SSD_CHUNK), dtype=bool))
    seg = jnp.exp(jnp.where(causal, a_cs[..., :, None] - a_cs[..., None, :], -jnp.inf))
    scores = jnp.einsum('bclgn,bcsgn->bcgls', cc, bc)
    y_diag = jnp.einsum('bcgjls,bcsgjp->bclgjp', scores[:, :, :, None] * seg, xc)
    decay_to_end = jnp.exp(a_cs[..., -1:] - a_cs)
    chunk_states = jnp.einsum('bclgn,bcgjl,bclgjp->bcgjpn', bc, decay_to_end, xc)
    chunk_decay = jnp.exp(a_cs[..., -1])

    def carry_state(s, inp):
        st, dec = inp
        return s * dec[..., None, None] + st, s

    s0 = jnp.zeros((bsz, SSD_GROUPS, hpg, hd, SSD_STATE), xc.dtype)
    _, s_in = lax.scan(carry_state, s0, (jnp.moveaxis(chunk_states, 1, 0), jnp.moveaxis(chunk_decay, 1, 0)))
    s_in = jnp.moveaxis(s_in, 0, 1)
    y_off = jnp.einsum('bclgn,bcgjpn,bcgjl->bclgjp', cc, s_in, jnp.exp(a_cs))
    return (y_diag + y_off).reshape(bsz, seq, n_heads, hd)

def mamba2_branch(pb, conv_w, conv_b, dt_bias, a_log, d_skip, norm_w):
    bsz, seq, _ = pb.shape
    z, xbc, dt = jnp.split(pb, [BRANCH_W, BRANCH_W + SSD_XBC], axis=-1)
    xbc = jax.nn.silu(causal_dwconv(xbc, conv_w) + conv_b)
    xs, bm, cm = jnp.split(xbc, [BRANCH_W, BRANCH_W + SSD_GROUPS * SSD_STATE], axis=-1)
    xs = xs.reshape(bsz, seq, SSD_HEADS, SSD_HEAD).astype(jnp.float32)
    bm = bm.reshape(bsz, seq, SSD_GROUPS, SSD_STATE).astype(jnp.float32)
    cm = cm.reshape(bsz, seq, SSD_GROUPS, SSD_STATE).astype(jnp.float32)
    dt = jax.nn.softplus(dt.astype(jnp.float32) + dt_bias)
    a = -jnp.exp(a_log.astype(jnp.float32))
    y = ssd_chunked(xs * dt[..., None], dt * a, bm, cm)
    y = y + d_skip[:, None] * xs
    y = y.reshape(bsz, seq, BRANCH_W) * jax.nn.silu(z.astype(jnp.float32))
    y = rmsnorm(y.reshape(bsz, seq, SSD_GROUPS, BRANCH_W // SSD_GROUPS),
                norm_w.reshape(SSD_GROUPS, BRANCH_W // SSD_GROUPS), SSD_NORM_EPS)
    return y.reshape(bsz, seq, BRANCH_W)

def short_conv_branch(pc, conv_w):
    bg, cg, xin, g = jnp.split(pc, 4, axis=-1)
    return bg * causal_dwconv(cg * xin, conv_w) * jax.nn.silu(g)

def setup_inputs(seed: int = 0) -> dict:
    key = jax.random.key(seed)
    ks = jax.random.split(key, 24)
    f32 = jnp.float32
    nrm = lambda k, shape, s: jax.random.normal(k, shape, f32) * s
    dt0 = jnp.exp(jax.random.uniform(ks[14], (DEPTH, SSD_HEADS), f32) * (np.log(0.1) - np.log(0.001)) + np.log(0.001))
    return {
        'x': nrm(ks[0], (BATCH, SEQ, D_MODEL), 1.0),
        'norm_w': 1.0 + nrm(ks[1], (DEPTH, D_MODEL), 0.05),
        'w_in': nrm(ks[2], (DEPTH, D_MODEL, IN_COLS), D_MODEL ** -0.5),
        'rw_mu': jax.random.uniform(ks[3], (DEPTH, RW_COLS), f32),
        'rw_w0': jax.random.uniform(ks[4], (DEPTH, BRANCH_W), f32, -6.0, 1.0),
        'rw_w2': nrm(ks[5], (DEPTH, RW_DECAY_RANK, BRANCH_W), 0.5 * RW_DECAY_RANK ** -0.5),
        'rw_a0': nrm(ks[6], (DEPTH, BRANCH_W), 0.5),
        'rw_a2': nrm(ks[7], (DEPTH, RW_AAA_RANK, BRANCH_W), 0.5 * RW_AAA_RANK ** -0.5),
        'rw_kk': 0.85 + nrm(ks[8], (DEPTH, BRANCH_W), 0.05),
        'rw_ka': 1.0 + nrm(ks[9], (DEPTH, BRANCH_W), 0.05),
        'rw_rk': nrm(ks[10], (DEPTH, RW_HEADS, RW_HEAD), 0.1),
        'rw_ln_w': 1.0 + nrm(ks[11], (DEPTH, BRANCH_W), 0.05),
        'rw_ln_b': nrm(ks[12], (DEPTH, BRANCH_W), 0.01),
        'ssd_conv_w': nrm(ks[13], (DEPTH, SSD_CONV, SSD_XBC), SSD_CONV ** -0.5),
        'ssd_conv_b': nrm(ks[15], (DEPTH, SSD_XBC), 0.01),
        'ssd_dt_bias': dt0 + jnp.log(-jnp.expm1(-dt0)),
        'ssd_a_log': jnp.log(jax.random.uniform(ks[16], (DEPTH, SSD_HEADS), f32, 1.0, 16.0)),
        'ssd_d': 1.0 + nrm(ks[17], (DEPTH, SSD_HEADS), 0.1),
        'ssd_norm_w': 1.0 + nrm(ks[18], (DEPTH, BRANCH_W), 0.05),
        'sc_conv_w': nrm(ks[19], (DEPTH, SC_CONV, BRANCH_W), SC_CONV ** -0.5),
        'w_branch': nrm(ks[20], (DEPTH, N_BRANCH, BRANCH_W, D_MODEL), BRANCH_W ** -0.5),
        'w_out': nrm(ks[21], (DEPTH, D_MODEL, D_MODEL), D_MODEL ** -0.5),
        'final_norm_w': 1.0 + nrm(ks[22], (D_MODEL,), 0.05),
    }

def reference(x, norm_w, w_in, rw_mu, rw_w0, rw_w2, rw_a0, rw_a2, rw_kk, rw_ka, rw_rk,
              rw_ln_w, rw_ln_b, ssd_conv_w, ssd_conv_b, ssd_dt_bias, ssd_a_log, ssd_d,
              ssd_norm_w, sc_conv_w, w_branch, w_out, final_norm_w):
    bsz, seq, _ = x.shape
    for l in range(DEPTH):
        h = rmsnorm(x, norm_w[l])
        p = h @ w_in[l]
        pa, pb, pc, pg = jnp.split(
            p, [RW_COLS, RW_COLS + SSD_COLS, RW_COLS + SSD_COLS + SC_COLS], axis=-1)
        oa = rwkv7_branch(pa, rw_mu[l], rw_w0[l], rw_w2[l], rw_a0[l], rw_a2[l], rw_kk[l],
                          rw_ka[l], rw_rk[l], rw_ln_w[l], rw_ln_b[l]).astype(x.dtype)
        ob = mamba2_branch(pb, ssd_conv_w[l], ssd_conv_b[l], ssd_dt_bias[l], ssd_a_log[l],
                           ssd_d[l], ssd_norm_w[l]).astype(x.dtype)
        oc = short_conv_branch(pc, sc_conv_w[l]).astype(x.dtype)
        o = jnp.stack([oa, ob, oc], axis=2)
        yb = jnp.einsum('btnw,nwd->btnd', o, w_branch[l])
        gates = jax.nn.sigmoid(pg.reshape(bsz, seq, N_BRANCH, D_MODEL))
        merged = jnp.sum(gates * yb, axis=2)
        x = x + merged @ w_out[l]
    return rmsnorm(x, final_norm_w)


_drawn_inputs = setup_inputs


def setup_inputs(seed=0):
    import zlib

    import numpy as np

    out = dict(_drawn_inputs(seed))
    spreads = {}
    factors = {'rw_w2': 8.0,
     'rw_kk': 28.144,
     'rw_ka': 4.437,
     'rw_ln_w': 5.436,
     'rw_ln_b': 41.175,
     'ssd_conv_b': 8.0,
     'ssd_d': 2.846,
     'ssd_norm_w': 3.939}
    for name, (base, spread) in spreads.items():
        noise = np.random.default_rng([zlib.crc32(name.encode()), seed]).standard_normal(out[name].shape)
        drawn = base * np.exp(spread * noise) if base else spread * noise
        out[name] = __import__('jax').numpy.asarray(drawn.astype(out[name].dtype))
    for name, factor in factors.items():
        out[name] = (out[name] * factor).astype(out[name].dtype)
    return out
```

```python
from contextlib import ExitStack

import numpy as np
import concourse.bass as bass
from concourse import mybir

F32 = mybir.dt.float32
F32R = mybir.dt.float32r
ALU = mybir.AluOpType
ACT = mybir.ActivationFunctionType
AX = mybir.AxisListType

P = 128
D = 2048
T = 256
W = 1024
KT = D // P
CT = W // P
NG, NS = 4, 128
RW0 = 0
RANKS = 4 * W
SSD0 = RANKS + 128
DT0 = SSD0 + 2 * W + 2 * NG * NS
SC0 = DT0 + 16
GATE0 = SC0 + 4 * W
EXP_M_HALF = float(np.exp(-0.5))
RING = 4
KC = 4
CW = 256
BLK = 16

MU, W0, A0, KK, KA, RK, LNW, LNB, NW, SNW = 0, 33, 41, 49, 57, 65, 73, 81, 89, 105
ROWS0 = 113
CVW, CVB, SCW = 128, 192, 208
ROWS1 = 104

PRE_STRIPS = 7
PRE = PRE_STRIPS * 4
ITER = 20
LAST = 12
MAIN_END = PRE + 7 * ITER + LAST
GATES = 6
GATE_END = MAIN_END + 3 * 8 * GATES
CHUNKS = GATE_END + 8 * 4
PRE_TILES = 2 * PRE_STRIPS
ITER_TILES = 10
LAST_TILES = 6
MAIN_TILES = PRE_TILES + 7 * ITER_TILES + LAST_TILES
SLOTS = 40
AHEAD = 2


def build_program(nc, x, norm_w, w_in, rw_mu, rw_w0, rw_w2, rw_a0, rw_a2, rw_kk, rw_ka, rw_rk, rw_ln_w, rw_ln_b,
                  ssd_conv_w, ssd_conv_b, ssd_dt_bias, ssd_a_log, ssd_d, ssd_norm_w, sc_conv_w, w_branch, w_out,
                  final_norm_w, out):
    ctx = ExitStack()
    with ctx:
        def sb(name, shape, dt=F32):
            return ctx.enter_context(nc.sbuf_tensor(name, shape, dt))

        def sem(name):
            return ctx.enter_context(nc.semaphore(name))

        raw = sb("raw", [P, RING, KC, CW])
        whi = sb("whi", [P, RING, KC, CW], F32R)
        wlo = sb("wlo", [P, RING, KC, CW], F32R)
        hhi = sb("hhi", [P, KT, T], F32R)
        hlo = sb("hlo", [P, KT, T], F32R)
        ohi = sb("ohi", [P, CT, T], F32R)
        olo = sb("olo", [P, CT, T], F32R)
        o = sb("o", [P, 2, CT, T])
        xtok = o[:, :, :, :].rearrange("p b j t -> p b (j t)")
        work = sb("work", [P, 4096])
        merged = work[:, :].rearrange("p (k t) -> p k t", k=KT)
        kdbd = work[:, 0:2048].rearrange("p (b w c n) -> p b w c n", b=2, w=2, c=4)
        s4 = work[:, 2048:4096].rearrange("p (q n) -> p q n", q=4)
        bc = work[:, 0:2048].rearrange("p (j t) -> p j t", j=8)
        fnw = work[:, 0:D]

        lots = sb("lots", [P, 44, T])

        def lot(a, n=1):
            return lots[:, a, :] if n == 1 else lots[:, a:a + n, :]

        def flat(a, n):
            return lots[:, a:a + n, :].rearrange("p a t -> p (a t)")

        sh = lot(0, 4)
        gg = lot(4, 3)
        kd = lot(7)
        qq = lot(4, 4)
        bd = lot(8)
        kk, k2, kh, bv = (lot(n) for n in range(9, 13))
        nm = flat(9, 4).rearrange("p (b e c n) -> p b e c n", b=2, e=2, c=4)
        dts = lots[0:16, 9:15, :]
        ksq, nrm, rin, bon = (lot(n) for n in range(13, 17))
        lshift = lot(15)
        prow = lot(16).rearrange("p (a c) -> p a c", a=2)
        kr = flat(17, 2).rearrange("p (b w t) -> p b w t", b=2, w=2)
        cv, cvt = lot(17), lot(18)
        tanhs = lot(19, 2)
        uu = flat(19, 2)
        xs2, xst = lot(19), lot(20).rearrange("p (b n) -> p b n", b=2)
        sga, ls, lp = lot(21, 2), lot(23), lot(24)
        seg = flat(21, 3).rearrange("p (e n) -> p e n", e=2)
        uw = flat(23, 2).rearrange("p (q n) -> p q n", q=4)
        vt = lot(25).rearrange("p (b n) -> p b n", b=2)
        xx = flat(26, 2)
        xx5 = xx.rearrange("p (b e w n) -> p b e w n", b=2, e=2, w=2)
        yz = flat(26, 2).rearrange("p (q n) -> p q n", q=4)
        tdt = flat(28, 2)
        ys, yc = lot(28), lot(29)
        yo, s2g = lot(30), lot(31)
        sol_n = lots[0:32, 32, :].rearrange("p (s t) -> p s t", s=BLK)
        sol_m = lots[0:32, 33, :]
        sol_t = lots[0:32, 34, :].rearrange("p (s t) -> p s t", s=BLK)
        scb = lot(35, 4)
        scc, scy, scf = lot(39), lot(40), lot(41)
        zp = lot(42, 2)
        sqs = lot(0, 8)
        sgt, gy = lot(8, 2), lot(10, 2)

        prm = sb("prm", [P, 256])
        omm = sb("omm", [P, 33])
        halfb = sb("halfb", [P, 16])
        dsk = sb("dsk", [P, CT])
        dskh = sb("dskh", [P, CT])
        ident = sb("ident", [P, P])
        mask4 = sb("mask4", [P, 4, P])
        m16s = sb("m16s", [P, P])
        m16i = sb("m16i", [P, P])
        head1 = sb("head1", [P, P])
        ones = sb("ones", [P, P])
        causal = sb("causal", [P, 384])
        restart = sb("restart", [P, T])
        eps3 = sb("eps3", [P, 3])
        lorat = sb("lorat", [P, 2, P])
        lr = sb("lr", [P, T])
        rowst = sb("rowst", [P, 6])
        pq = sb("pq", [P, 4, 1 + T])
        adt = sb("adt", [P, P])
        ad = sb("ad", [P, 4, BLK])
        tc = sb("tc", [P, 4, BLK])
        st = sb("st", [P, 2, 8, 64])
        gcs = sb("gcs", [P, 2, 8])
        scx = sb("scx", [P, 2 + T])
        xp = sb("xp", [P, 3 + T])
        scm = sb("scm", [P, NG, 384])
        dtc = sb("dtc", [16, 4])
        acs = sb("acs", [16, T])
        acm = sb("acm", [16, 2, T])
        dat = sb("dat", [P, 2, 2, 16])

        ps = ctx.enter_context(nc.psum_tensor("ps", [P, 8, 512], F32))
        A, B, C, E = (ps[:, n, :] for n in range(4, 8))
        BANKS = (0, 2, 0, 0, 2)

        scr_n = nc.dram_tensor("scr_n", [32, BLK, BLK], F32, kind="Internal").ap()
        scr_t = nc.dram_tensor("scr_t", [32, BLK, BLK], F32, kind="Internal").ap()

        x_in, prm_in, lora_in, dtp_in, dsk_in = (sem(n) for n in ("x_in", "prm_in", "lora_in", "dtp_in", "dsk_in"))
        raw_in = [sem(f"raw_in{n}") for n in range(RING)]
        hi_done, lo_done, chunk_used = sem("hi_done"), sem("lo_done"), sem("chunk_used")
        tile_done, tile_out, y_done = sem("tile_done"), sem("tile_out"), sem("y_done")
        names = """kdbd_z const_z const_m const_o prm_t prm_ok prm_d x_sq x_rt x_rs x_n x_tr h_hi h_lo
            ranks_sh lr_ok bc_s bc_th bc_ok sc_mm scm_ok dt_x
            dt_ab dt_e dt_u dt_l dt_d dt_i dt_r dt_c dt_ok dt_ae dt_da acs_ok dt_tr dat_ok
            shifted lora_mm tanh_wa sig_wa cum cum_prev exps kk_ok kk_sq kk_mm kk_max kk_rt kk_rin kh_ok
            ka_t k2_ok rk_ok rk_mm bon_ok bv_ok prod_ok tr_vk tr_kb vt_ok kdbd_ok
            score_mm score_ok adt_ok ad_ok ad_out n_in sol_p sol_r t_out t_in tdt_ok xv_mm xv_ok u_mm u_ok
            ou_mm xo_ok uw_mm uw_ok yz_mm yz_ok nm_mm nm_ok gc_mm gc_ok state_mm state_ok y_mm ys_ok mean_mm yc_ok
            ysq_ok var_mm var_rt var_r yn_ok yl_ok yb_ok g_th g2_ok oa_ok
            sc_cx sc_s sc_g2 sc_b sc_f oc_hi oc_ok
            x_s x_th xs_ok z2_ok x_tr2 xst_ok acm_ok acb_mm seg_ok seg_e seg_g yb_mm ob_d ob_ok
            sq_ok gn_mm gn_rt gn_r gn_ok osp_hi osp_lo gy_ok mg_ok m_hi m_lo
            out_mm out_ok f_sq f_m f_rt f_rs f_ok stored"""
        s = {n: sem(n) for n in names.split()}

        block = ctx.enter_context(nc.Block())

        @block.sync
        def _(sp):
            for b in range(2):
                sp.dma_start(xtok[:, b, :], x[0, b * P:(b + 1) * P, :]).then_inc(x_in, 16)

            def slot_free(c):
                sp.wait_ge(lo_done, c - (RING - 1))

            def strip(c, cols, widths=(P, P), first=False):
                for q in range(4):
                    if not first:
                        slot_free(c + q)
                    for at, c0, w in ((0, cols[0], widths[0]), (P, cols[1], widths[1])):
                        src = w_in[0, q * KC * P:(q + 1) * KC * P, bass.ds(c0, w)].rearrange("(k p) c -> p k c", p=P)
                        sp.dma_start(raw[:, q, :, at:at + w], src).then_inc(raw_in[q], 16)

            def block_chunk(c, slot, src):
                slot_free(c)
                for half in (1, 0):
                    sp.dma_start(raw[:, slot, 2 * half:2 * half + 2, :],
                                 src(half * 2 * P, (half + 1) * 2 * P).rearrange("(k p) c -> p k c", p=P)
                                 ).then_inc(raw_in[slot], 16)

            def load_lora(j):
                sp.dma_start(lorat[0:64, 0, :], rw_w2[0, :, bass.ds(j * P, P)]).then_inc(lora_in, 16)
                sp.dma_start(lorat[64:128, 1, :], rw_a2[0, :, bass.ds(j * P, P)]).then_inc(lora_in, 16)

            strip(0, (RANKS, DT0), (P, 16), first=True)
            sp.wait_ge(s["const_z"], 2)
            load_lora(0)
            for n in range(4):
                c0 = SSD0 + 2 * W + n * 256
                strip(4 + 4 * n, (c0, c0 + P))
            strip(20, (0, W))
            strip(24, (2 * W, 3 * W))

            def main(j, last):
                c = PRE + j * ITER
                strip(c, (SC0 + j * P, SC0 + W + j * P))
                strip(c + 4, (SC0 + 2 * W + j * P, SC0 + 3 * W + j * P))
                strip(c + 8, (SSD0 + W + j * P, SSD0 + j * P))
                if not last:
                    sp.wait_ge(s["lora_mm"], j + 1)
                    load_lora(j + 1)
                    strip(c + 12, ((j + 1) * P, W + (j + 1) * P))
                    strip(c + 16, (2 * W + (j + 1) * P, 3 * W + (j + 1) * P))

            with sp.Fori(0, CT - 1) as j:
                main(j, False)
            main(CT - 1, True)

            for n in range(3):
                br = 2 - n
                base = MAIN_END + n * 8 * GATES
                with sp.Fori(0, 4) as i:
                    for h in range(2):
                        col = i * (2 * CW) + h * CW
                        for q in range(GATES):
                            if q < 4:
                                def src(a, b):
                                    return w_in[0, q * KC * P + a:q * KC * P + b, bass.ds(col + GATE0 + br * D, CW)]
                            else:
                                def src(a, b):
                                    return w_branch[0, br, (q - 4) * KC * P + a:(q - 4) * KC * P + b, bass.ds(col, CW)]
                            y = h * GATES + q
                            block_chunk(base + i * (2 * GATES) + y, (base + y) % RING, src)
            sp.wait_ge(s["osp_lo"], 4)
            for b in range(2):
                sp.dma_start(xtok[:, b, :], x[0, b * P:(b + 1) * P, :]).then_inc(x_in, 16)
            with sp.Fori(0, 4) as i:
                for h in range(2):
                    for q in range(4):
                        block_chunk(GATE_END + i * 8 + h * 4 + q, q,
                                    lambda a, b: w_out[0, q * KC * P + a:q * KC * P + b, bass.ds(i * (2 * CW) + h * CW, CW)])
            sp.wait_ge(s["m_lo"], 4)
            sp.dma_start(fnw, final_norm_w.rearrange("(a n) -> a n", a=1).broadcast_to([P, D])).then_inc(x_in, 16)
            for b in range(2):
                sp.wait_ge(s["f_ok"], b + 1)
                sp.dma_start(out[0, b * P:(b + 1) * P, :], xtok[:, b, :]).then_inc(s["stored"], 16)
            sp.wait_ge(s["stored"], 32)

        @block.gpsimd
        def _(pool):
            gp = nc.gpsimd
            for t, v in ((ident[:], 0.0), (mask4[:], 1.0), (m16s[:], 1.0), (m16i[:], 1.0), (head1[:], 1.0),
                         (ones[:], 1.0), (causal[:], 0.25), (restart[:], 1.0), (st[:], 0.0), (sol_t, 0.0),
                         (lorat[:], 0.0), (pq[:], 0.0), (xp[:], 0.0), (scx[:], 0.0), (eps3[:, 0:1], 1e-6),
                         (eps3[:, 1:2], 64e-5)):
                gp.memset(t, v)
            gp.memset(eps3[:, 2:3], 1e-5).then_inc(s["const_z"], 1)
            pool.wait_ge(s["const_z"], 1)
            gp.affine_select(out=ident[:], in_=ident[:], compare_op=ALU.not_equal, fill=1.0, base=0,
                             pattern=[[-1, P]], channel_multiplier=1)
            gp.affine_select(out=sol_t, in_=sol_t, compare_op=ALU.not_equal, fill=1.0, base=0,
                             pattern=[[1, BLK], [-1, BLK]], channel_multiplier=0)
            for m, base in ((mask4[:, 0, :], -1), (mask4[:, 1, :], 0), (m16s[:], -1), (m16i[:], 0),
                            (causal[:, 0:P], 0), (causal[:, 256:384], 0)):
                gp.affine_select(out=m, in_=m, compare_op=ALU.is_ge, fill=0.0, base=base,
                                 pattern=[[1, P]], channel_multiplier=-1)
            h1 = head1[:].rearrange("p (e u) -> p e u", e=2)
            gp.affine_select(out=h1, in_=h1, compare_op=ALU.is_ge, fill=0.0, base=0,
                             pattern=[[-64, 2], [0, 64]], channel_multiplier=1).then_inc(s["const_z"], 1)
            pool.wait_ge(s["const_z"], 2)
            for m, n in ((mask4[:, 0, :], 4), (mask4[:, 1, :], 4), (m16s[:], 8), (m16i[:], 8)):
                v = m.rearrange("p (b u) -> p b u", b=n)
                gp.affine_select(out=v, in_=v, compare_op=ALU.is_ge, fill=0.0, base=0,
                                 pattern=[[-(P // n), n], [0, P // n]], channel_multiplier=1)
            gp.affine_select(out=h1, in_=h1, compare_op=ALU.is_ge, fill=0.0, base=63,
                             pattern=[[64, 2], [0, 64]], channel_multiplier=-1)
            gp.memset(restart[:].rearrange("p (c u) -> p c u", u=32)[:, :, 0:1], 0.0).then_inc(s["const_m"], 1)

            def main(j):
                pool.wait_ge(s["kk_ok"], j + 1)
                gp.tensor_tensor(ksq, kk, kk, ALU.mult).then_inc(s["kk_sq"], 1)
                pool.wait_ge(s["cum"], j + 1)
                gp.tensor_tensor(lp, ls, sga[:, 0, :], ALU.subtract).then_inc(s["cum_prev"], 1)
                pool.wait_ge(s["kk_rin"], j + 1)
                gp.tensor_tensor(kh, kk, rin, ALU.mult).then_inc(s["kh_ok"], 1)
                pool.wait_ge(s["kh_ok"], j + 1)
                gp.tensor_tensor(bv, kh, sga[:, 1, :], ALU.mult).then_inc(s["bv_ok"], 1)
                pool.wait_ge(tile_out, j * ITER_TILES + PRE_TILES + 4)
                gp.tensor_tensor(scx[:, 2:2 + T], scb[:, 1, :], scb[:, 2, :], ALU.mult).then_inc(s["sc_cx"], 1)
                pool.wait_ge(s["yc_ok"], j + 1)
                gp.tensor_tensor(ksq, yc, yc, ALU.mult).then_inc(s["ysq_ok"], 1)

            pool.wait_ge(s["sc_mm"], NG)
            gp.memset(kdbd, 0.0).then_inc(s["kdbd_z"], 1)

            with gp.Fori(0, CT - 1) as j:
                main(j)
            main(CT - 1)
            pool.wait_ge(s["ob_ok"], CT)
            pool.wait_ge(s["oa_ok"], CT)
            for j in range(CT):
                last = gp.tensor_tensor(sqs[:, j, :], o[:, 1, j, :], o[:, 1, j, :], ALU.mult)
            last.then_inc(s["sq_ok"], 1)

        @block.scalar
        def _(act):
            sc = nc.scalar
            by_tile = "a (r c) -> (a r) c"
            rows = [(MU, rw_mu.rearrange(by_tile, c=P)), (W0, rw_w0.rearrange(by_tile, c=P)),
                    (A0, rw_a0.rearrange(by_tile, c=P)), (KK, rw_kk.rearrange(by_tile, c=P)),
                    (KA, rw_ka.rearrange(by_tile, c=P)), (RK, rw_rk.rearrange("a (r e) c -> (a r) (e c)", e=2)),
                    (LNW, rw_ln_w.rearrange(by_tile, c=P)), (LNB, rw_ln_b.rearrange(by_tile, c=P)),
                    (NW, norm_w.rearrange(by_tile, c=P)), (SNW, ssd_norm_w.rearrange(by_tile, c=P)),
                    (CVW, ssd_conv_w.rearrange("a k (r c) -> (a k r) c", c=P)),
                    (CVB, ssd_conv_b.rearrange(by_tile, c=P)),
                    (SCW, sc_conv_w.rearrange("a k (r c) -> (a k r) c", c=P))]
            for r0, src in rows:
                act.dma_start(prow[r0 % P:r0 % P + src.shape[0], r0 // P, :], src).then_inc(prm_in, 16)
            act.dma_start(dtc[:, 0:1], ssd_dt_bias.rearrange("a h -> h a"), allow_slow_non_contiguous=True).then_inc(dtp_in, 16)
            act.dma_start(dtc[:, 1:2], ssd_a_log.rearrange("a h -> h a"), allow_slow_non_contiguous=True).then_inc(dtp_in, 16)
            by_head = ssd_d.rearrange("a (j e) -> e a j", e=2)
            for e in range(2):
                act.dma_start(dsk[64 * e:64 * e + 64, :], by_head[e].broadcast_to([64, CT]),
                              allow_slow_non_contiguous=True).then_inc(dsk_in, 16)

            act.wait_ge(x_in, 32)
            for b in range(2):
                sc.activation(work[:, b * D:(b + 1) * D], xtok[:, b, :], ACT.Square,
                              accum_out=rowst[:, b:b + 1]).then_inc(s["x_sq"], 1)
            act.wait_ge(s["const_z"], 2)
            act.wait_ge(s["x_sq"], 2)
            sc.activation(rowst[:, 2:4], rowst[:, 0:2], ACT.Sqrt, scale=1.0 / D, bias=eps3[:, 0:1]).then_inc(s["x_rt"], 1)
            act.wait_ge(s["prm_t"], 1)
            sc.activation(prm[:, 0:ROWS0], A[:, 0:ROWS0], ACT.Copy)
            sc.activation(prm[:, P:P + ROWS1], A[:, P:P + ROWS1], ACT.Copy).then_inc(s["prm_ok"], 1)
            act.wait_ge(s["prm_ok"], 1)
            for k in range(KT):
                act.wait_ge(s["x_tr"], k + 1)
                sc.activation(hhi[:, k, :], ps[:, 4 + k % 4, 0:T], ACT.Copy,
                              scale=prm[:, NW + k:NW + k + 1]).then_inc(s["h_hi"], 1)

            def split_hi(c, slot, use, width=CW, first=False):
                act.wait_ge(raw_in[slot], use * 32)
                if not first:
                    act.wait_ge(chunk_used, c - (RING - 1))
                sc.activation(whi[:, slot, :, 0:width], raw[:, slot, :, 0:width], ACT.Copy).then_inc(hi_done, 1)

            def proj(strip, t, bank, dst):
                if t == 0:
                    act.wait_ge(tile_done, strip + 1)
                else:
                    act.wait_ge(chunk_used, strip * 4 + 4)
                return sc.activation(dst, ps[:, bank, 0:T], ACT.Copy)

            def shift_pair(j, a, bank, strip):
                for t in range(2):
                    w = 2 * a + t
                    proj(strip, t, bank + t, pq[:, w, 1:1 + T])
                    sc.activation(qq[:, w, :], ps[:, bank + t, 0:T], ACT.Copy,
                                  scale=omm[:, bass.ds(j + w * CT, 1)]).then_inc(tile_out, 1)

            for c in range(AHEAD):
                split_hi(c, c, 1, P + 16, first=True)
            act.wait_ge(s["prm_d"], 1)
            for c in range(PRE):
                n = c + AHEAD
                if n < PRE:
                    split_hi(n, n % RING, n // RING + 1, P + 16 if n < 4 else CW, first=n < RING)
                if c == 4:
                    act.wait_ge(s["const_m"], 1)
                    proj(0, 0, 2, pq[:, 0, 1:1 + T])
                    sc.activation(qq[:, 0, :], ps[:, 2, 0:T], ACT.Copy, scale=omm[:, 32:33]).then_inc(tile_out, 1)
                    act.wait_ge(chunk_used, 4)
                    act.wait_ge(dtp_in, 32)
                    sc.activation(dts[:, 0, :], ps[0:16, 3, 0:T], ACT.Identity, bias=dtc[:, 0:1]).then_inc(tile_out, 1)
                if c % 4 == 0 and 8 <= c <= 20:
                    for t in range(2):
                        m = 2 * (c // 4 - 2) + t
                        if m >= 1:
                            act.wait_ge(s["bc_s"], 4 * m)
                        proj(c // 4 - 1, t, 2 * ((c // 4) % 2) + t, xp[:, 3:3 + T]).then_inc(tile_out, 1)
                        act.wait_ge(s["bc_s"], 4 * m + 4)
                        sc.activation(cvt, cv, ACT.Tanh, scale=0.5).then_inc(s["bc_th"], 1)
                if c == 24:
                    act.wait_ge(s["ranks_sh"], 1)
                    sc.activation(lr[0:64, :], lshift[0:64, :], ACT.Tanh)
                    sc.activation(lr[64:128, :], lshift[64:128, :], ACT.Copy).then_inc(s["lr_ok"], 1)
                    act.wait_ge(s["dt_ab"], 1)
                    sc.activation(dts[:, 2, :], dts[:, 1, :], ACT.Exp, scale=-1.0).then_inc(s["dt_e"], 1)
                    sc.activation(dtc[:, 2:3], dtc[:, 1:2], ACT.Exp).then_inc(s["dt_ae"], 1)
                    act.wait_ge(s["dt_u"], 1)
                    sc.activation(dts[:, 4, :], dts[:, 3, :], ACT.Ln).then_inc(s["dt_l"], 1)
                    shift_pair(0, 0, 0, 5)
            act.wait_ge(s["dt_tr"], 1)
            sc.activation(dat[:].rearrange("p w b h -> p (w b h)"), B[:, 0:64], ACT.Copy).then_inc(s["dat_ok"], 1)

            def main(j, last):
                base = PRE + j * ITER
                strip0 = PRE_STRIPS + j * 5
                nchunks = LAST if last else ITER

                def split(c):
                    split_hi(base + c, c % RING, PRE // RING + j * (ITER // RING) + c // RING + 1)

                for t in range(SLOTS):
                    if t == 0:
                        for c in range(AHEAD):
                            split(c)
                        shift_pair(j, 1, BANKS[4], strip0 - 1)
                    if t % 2 == 0 and t // 2 + AHEAD < nchunks:
                        split(t // 2 + AHEAD)
                    if t == 1:
                        act.wait_ge(s["lora_mm"], j + 1)
                        sc.activation(tanhs[:, 0, :], A[:, 0:T], ACT.Tanh, scale=0.5, bias=halfb[:, bass.ds(j, 1)])
                        sc.activation(tanhs[:, 1, :], A[:, T:2 * T], ACT.Tanh, scale=0.5,
                                      bias=halfb[:, bass.ds(j + CT, 1)]).then_inc(s["tanh_wa"], 1)
                        act.wait_ge(s["shifted"], j * 4 + 4)
                        sc.activation(s2g, sh[:, 3, :], ACT.Tanh, scale=0.5).then_inc(s["g_th"], 1)
                    if t == 3:
                        act.wait_ge(s["cum"], j + 1)
                        sc.activation(gg[:, 0, :], ls, ACT.Exp, scale=-EXP_M_HALF)
                        sc.activation(gg[:, 1, :], ls, ACT.Exp, scale=EXP_M_HALF)
                        act.wait_ge(s["cum_prev"], j + 1)
                        sc.activation(gg[:, 2, :], lp, ACT.Exp, scale=-EXP_M_HALF).then_inc(s["exps"], 1)
                        act.wait_ge(s["kk_max"], j + 1)
                        sc.activation(nrm, ksq, ACT.Sqrt).then_inc(s["kk_rt"], 1)
                    if t == 7:
                        act.wait_ge(s["tr_vk"], j + 1)
                        cvk = C.rearrange("p (b w n) -> p b w n", b=2, w=2)
                        sc.activation(vt, cvk[:, :, 0, :], ACT.Copy)
                        sc.activation(xx5[:, :, :, 1, :], cvk[:, :, 1, :].rearrange("p b (e n) -> p b e n", e=2),
                                      ACT.Copy).then_inc(s["vt_ok"], 1)
                        act.wait_ge(s["tr_kb"], j + 1)
                        act.wait_ge(s["kdbd_z"], 1)
                        dkb = E.rearrange("p (b w n) -> p b w n", b=2, w=2)
                        for c in range(4):
                            r = slice(32 * c, 32 * c + 32)
                            op = sc.activation(kdbd[r, :, :, c, :], dkb[r, :, :, :], ACT.Copy)
                        op.then_inc(s["kdbd_ok"], 1)
                    if t == 8:
                        proj(strip0, 0, BANKS[0], scb[:, 0, :]).then_inc(tile_out, 1)
                        proj(strip0, 1, BANKS[0] + 1, scb[:, 1, :]).then_inc(tile_out, 1)
                    if t == 9:
                        act.wait_ge(s["ad_ok"], j * 4 + 4)
                        act.dma_start(scr_n.rearrange("(q b) s t -> (b s) q t", q=4), ad[:]).then_inc(s["ad_out"], 16)
                    if t == 12:
                        act.wait_ge(s["ad_out"], j * 16 + 16)
                        act.dma_start(sol_n, scr_n).then_inc(s["n_in"], 16)
                    if t == 15:
                        act.wait_ge(s["sol_r"], j * 15 + 15)
                        act.dma_start(scr_t, sol_t).then_inc(s["t_out"], 16)
                    if t == 17:
                        act.wait_ge(s["t_out"], j * 16 + 16)
                        act.dma_start(tc[:], scr_t.rearrange("(q b) s t -> (b s) q t", q=4)).then_inc(s["t_in"], 16)
                    if t == 11:
                        act.wait_ge(s["xv_mm"], j + 1)
                        sc.activation(xx5[:, :, :, 0, :], E[:, 0:T].rearrange("p (b e n) -> p b e n", b=2, e=2),
                                      ACT.Copy).then_inc(s["xv_ok"], 1)
                    if t == 16:
                        proj(strip0 + 1, 0, BANKS[1], scb[:, 2, :]).then_inc(tile_out, 1)
                        proj(strip0 + 1, 1, BANKS[1] + 1, scb[:, 3, :])
                        sc.activation(scc, ps[:, BANKS[1] + 1, 0:T], ACT.Tanh, scale=0.5).then_inc(tile_out, 1)
                    if t == 18:
                        act.wait_ge(s["sc_f"], j + 1)
                        sc.activation(ohi[:, bass.ds(j, 1), :], scf.unsqueeze(1), ACT.Copy).then_inc(s["oc_hi"], 1)
                    if t == 19:
                        act.wait_ge(s["u_mm"], j + 1)
                        sc.activation(uu, B, ACT.Copy).then_inc(s["u_ok"], 1)
                    if t == 21:
                        act.wait_ge(s["uw_mm"], j + 1)
                        sc.activation(uw.rearrange("p q n -> p (q n)"), B, ACT.Copy).then_inc(s["uw_ok"], 1)
                    if t == 23:
                        act.wait_ge(s["yz_mm"], j + 1)
                        sc.activation(yz.rearrange("p q n -> p (q n)"), A, ACT.Copy).then_inc(s["yz_ok"], 1)
                    if t == 24:
                        act.wait_ge(s["gc_mm"], j + 1)
                        sc.activation(gcs[64:128, :, :], B[64:128, 0:16].rearrange("p (e c) -> p e c", e=2),
                                      ACT.Copy).then_inc(s["gc_ok"], 1)
                        proj(strip0 + 2, 0, BANKS[2], xp[:, 3:3 + T]).then_inc(tile_out, 1)
                        proj(strip0 + 2, 1, BANKS[2] + 1, zp[:, 0, :])
                        sc.activation(zp[:, 1, :], ps[:, BANKS[2] + 1, 0:T], ACT.Tanh, scale=0.5).then_inc(tile_out, 1)
                    if t == 26:
                        act.wait_ge(s["x_s"], j * 4 + 4)
                        sc.activation(cvt, cv, ACT.Tanh, scale=0.5).then_inc(s["x_th"], 1)
                    if t == 28:
                        act.wait_ge(s["x_tr2"], j + 1)
                        sc.activation(xst.rearrange("p b n -> p (b n)"), C[:, 0:T], ACT.Copy,
                                      scale=0.5).then_inc(s["xst_ok"], 1)
                        act.wait_ge(s["seg_ok"], j + 1)
                        sc.activation(seg, seg, ACT.Exp).then_inc(s["seg_e"], 1)
                    if t == 32:
                        act.wait_ge(s["y_mm"], j + 1)
                        sc.activation(ys, B[:, 0:T], ACT.Copy).then_inc(s["ys_ok"], 1)
                        if not last:
                            shift_pair(j + 1, 0, BANKS[3], strip0 + 3)
                    if t == 35:
                        act.wait_ge(s["var_mm"], j + 1)
                        sc.activation(nrm, C[:, 0:T], ACT.Sqrt, scale=1.0 / 64, bias=eps3[:, 1:2]).then_inc(s["var_rt"], 1)

            with act.Fori(0, CT - 1) as j:
                main(j, False)
            main(CT - 1, True)

            for c in range(AHEAD):
                split_hi(MAIN_END + c, (MAIN_END + c) % RING, (MAIN_END + c) // RING + 1)
            for n in range(3):
                base = MAIN_END + n * 8 * GATES
                if n > 0:
                    act.wait_ge(s["gn_ok"] if n == 1 else s["oa_ok"], CT)
                    act.wait_ge(chunk_used, base)
                    for half in range(2):
                        r = slice(4 * half, 4 * half + 4)
                        sc.activation(ohi[:, r, :], o[:, 2 - n, r, :], ACT.Copy).then_inc(s["osp_hi"], 1)

                def gates(i, peeled, tail):
                    for h in range(2):
                        for q in range(GATES):
                            y = h * GATES + q + AHEAD
                            if not (tail and y >= 2 * GATES):
                                split_hi(base + i * (2 * GATES) + y, (base + y) % RING,
                                         (base + y) // RING + 1 + i * (2 * GATES // RING))
                            if q == 4:
                                for t in range(2):
                                    g = 16 * n + i * 4 + 2 * h + t
                                    strip = i * 2 + (8 * n + h)
                                    if t == 0:
                                        act.wait_ge(tile_done, strip + MAIN_TILES // 2 + 1)
                                    else:
                                        act.wait_ge(chunk_used, strip * GATES + MAIN_END + 4)
                                    if not (peeled and h == 0):
                                        act.wait_ge(s["gy_ok"], g - 1)
                                    sc.activation(sgt[:, t, :], ps[:, 2 + t, 0:T], ACT.Sigmoid).then_inc(tile_out, 1)

                if n == 0:
                    act.wait_ge(s["oa_ok"], CT)
                    gates(0, True, False)
                    act.wait_ge(s["gn_mm"], 4)
                    for g in range(4):
                        sc.activation(sqs[:, g, :], ps[:, 4 + g, 0:T], ACT.Sqrt, scale=1.0 / 256,
                                      bias=eps3[:, 2:3]).then_inc(s["gn_rt"], 1)
                with act.Fori(1 if n == 0 else 0, 3) as i:
                    gates(i, False, False)
                gates(3, False, n == 2)
            act.wait_ge(chunk_used, GATE_END - 2)
            act.wait_ge(s["mg_ok"], 32)
            for k in range(4):
                sc.activation(hhi[:, 4 * k:4 * k + 4, :], merged[:, 4 * k:4 * k + 4, :], ACT.Copy).then_inc(s["m_hi"], 1)
            for k in range(AHEAD):
                split_hi(GATE_END + k, k, GATE_END // RING + 1)

            def outs(i, tail):
                for y in range(AHEAD, 8 + AHEAD):
                    if not (tail and y >= 8):
                        split_hi(GATE_END + i * 8 + y, y % RING, GATE_END // RING + 1 + i * 2 + y // RING)

            with act.Fori(0, 3) as i:
                outs(i, False)
            outs(3, True)
            act.wait_ge(s["out_ok"], 16)
            for b in range(2):
                if b:
                    act.wait_ge(s["f_sq"], 1)
                sc.activation(work[:, D:2 * D], xtok[:, b, :], ACT.Square, accum_out=rowst[:, b:b + 1]).then_inc(s["f_sq"], 1)
            act.wait_ge(s["f_sq"], 2)
            sc.activation(rowst[:, 2:4], rowst[:, 0:2], ACT.Sqrt, scale=1.0 / D, bias=eps3[:, 0:1]).then_inc(s["f_rt"], 1)

        @block.vector
        def _(dve):
            v = nc.vector
            tt, ts, stt = v.tensor_tensor, v.tensor_scalar, v.scalar_tensor_tensor

            dve.wait_ge(s["x_rt"], 1)
            v.reciprocal(rowst[:, 4:6], rowst[:, 2:4]).then_inc(s["x_rs"], 1)
            dve.wait_ge(s["x_rs"], 1)
            for b in range(2):
                ts(xtok[:, b, :], xtok[:, b, :], rowst[:, 4 + b:5 + b], None, ALU.mult).then_inc(s["x_n"], 1)
            dve.wait_ge(s["const_m"], 1)
            v.tensor_copy(st[0:64, :, :, :].rearrange("p e c n -> p (e c) n"),
                          ident[0:64, 0:64].unsqueeze(1).broadcast_to([64, 16, 64]))
            v.tensor_copy(mask4[:, 3, :], mask4[:, 1, :])
            tt(mask4[:, 2, :], mask4[:, 0, :], m16s[:], ALU.subtract).then_inc(s["const_o"], 1)
            dve.wait_ge(s["prm_ok"], 1)
            ts(omm[:], prm[:, MU:MU + 33], -1.0, 1.0, ALU.mult, ALU.add)
            dve.wait_ge(dsk_in, 32)
            ts(dskh[:], dsk[:], 0.5, None, ALU.mult)
            ts(halfb[:], prm[:, W0:W0 + 16], 0.5, None, ALU.mult).then_inc(s["prm_d"], 1)
            for k in range(KT):
                dve.wait_ge(s["h_hi"], k + 1)
                stt(hlo[:, k, :], ps[:, 4 + k % 4, 0:T], prm[:, NW + k:NW + k + 1], hhi[:, k, :].bitcast(F32),
                    ALU.mult, ALU.subtract).then_inc(s["h_lo"], 1)

            def split_lo(c, slot, width=CW):
                dve.wait_ge(hi_done, c + 1)
                tt(wlo[:, slot, :, 0:width], raw[:, slot, :, 0:width], whi[:, slot, :, 0:width].bitcast(F32),
                   ALU.subtract).then_inc(lo_done, 1)

            def conv4(done, at, ch):
                for k in range(4):
                    tap = prm[:, bass.ds(ch + (CVW + 16 * k), 1)]
                    if k:
                        dve.wait_ge(done, at + k)
                        op = stt(cv, xp[:, k:k + T], tap, cv, ALU.mult, ALU.add)
                    else:
                        op = ts(cv, xp[:, 0:T], tap, prm[:, bass.ds(ch + CVB, 1)], ALU.mult, ALU.add)
                    op.then_inc(done, 1)

            for c in range(AHEAD):
                split_lo(c, c, P + 16)
            for c in range(PRE):
                n = c + AHEAD
                if n < PRE:
                    split_lo(n, n % RING, P + 16 if n < 4 else CW)
                if c == 4:
                    dve.wait_ge(tile_out, 1)
                    stt(lshift, pq[:, 0, 0:T], prm[:, MU + 32:MU + 33], qq[:, 0, :], ALU.mult, ALU.add
                        ).then_inc(s["ranks_sh"], 1)
                    dve.wait_ge(tile_out, 2)
                    stt(dts[:, 1, :], dts[:, 0, :], -1.0, dts[:, 0, :], ALU.mult, ALU.max).then_inc(s["dt_ab"], 1)
                if c % 4 == 0 and 8 <= c <= 20:
                    for t in range(2):
                        m = 2 * (c // 4 - 2) + t
                        dve.wait_ge(tile_out, 3 + m)
                        conv4(s["bc_s"], 4 * m, 8 + m)
                        dve.wait_ge(s["bc_th"], m + 1)
                        stt(bc[:, m, :], cvt, 1.0, cv, ALU.add, ALU.mult).then_inc(s["bc_ok"], 1)
                        dve.wait_ge(s["bc_ok"], m + 1)
                if c == 24:
                    dve.wait_ge(s["dt_e"], 1)
                    ts(dts[:, 3, :], dts[:, 2, :], 1.0, None, ALU.add).then_inc(s["dt_u"], 1)
                    dve.wait_ge(s["dt_u"], 1)
                    stt(dts[:, 1, :], dts[:, 3, :], -1.0, dts[:, 2, :], ALU.add, ALU.subtract).then_inc(s["dt_d"], 1)
                    v.reciprocal(dts[:, 5, :], dts[:, 3, :]).then_inc(s["dt_i"], 1)
                    dve.wait_ge(s["dt_i"], 1)
                    dve.wait_ge(s["dt_d"], 1)
                    tt(dts[:, 2, :], dts[:, 1, :], dts[:, 5, :], ALU.mult).then_inc(s["dt_r"], 1)
                    dve.wait_ge(s["dt_r"], 1)
                    dve.wait_ge(s["dt_l"], 1)
                    tt(dts[:, 1, :], dts[:, 4, :], dts[:, 2, :], ALU.subtract).then_inc(s["dt_c"], 1)
                    dve.wait_ge(s["dt_c"], 1)
                    stt(dts[:, 5, :], dts[:, 0, :], 0.0, dts[:, 1, :], ALU.max, ALU.add).then_inc(s["dt_ok"], 1)
                    dve.wait_ge(s["dt_ok"], 1)
                    dve.wait_ge(s["dt_ae"], 1)
                    ts(dts[:, 3, :], dts[:, 5, :], dtc[:, 2:3], -1.0, ALU.mult, ALU.mult).then_inc(s["dt_da"], 1)
                    dve.wait_ge(s["dt_da"], 1)
                    v.tensor_tensor_scan(acs[:], ones[0:16, 0:1].broadcast_to([16, T]), dts[:, 3, :], 0.0,
                                         ALU.mult, ALU.add).then_inc(s["acs_ok"], 1)
                    for g in range(NG):
                        dve.wait_ge(s["sc_mm"], g + 1)
                        tt(scm[:, g, :], ps[:, 4 + g, 0:384], causal[:], ALU.mult).then_inc(s["scm_ok"], 1)

            def main(j, last):
                base = PRE + j * ITER
                nt = PRE_TILES + j * ITER_TILES
                nchunks = LAST if last else ITER

                def col(at):
                    return prm[:, bass.ds(j + at, 1)]

                def scores(b):
                    for e in range(2):
                        q = 2 * b + e
                        dve.wait_ge(s["score_mm"], j * 4 + q + 1)
                        src = ps[:, 4 + e, :]
                        tt(adt[:], src[:, 256:384], m16s[:], ALU.mult).then_inc(s["adt_ok"], 1)
                        tt(s4[:, q, :], src, mask4[:].rearrange("p a t -> p (a t)"), ALU.mult).then_inc(s["score_ok"], 1)
                        dve.wait_ge(s["adt_ok"], j * 4 + q + 1)
                        v.tensor_reduce(ad[:, q, :], adt[:].rearrange("p (b u) -> p u b", u=BLK), AX.X, ALU.add
                                        ).then_inc(s["ad_ok"], 1)
                        dve.wait_ge(s["ad_ok"], j * 4 + q + 1)

                def solve(lo, hi):
                    for k in range(lo, hi):
                        r = BLK - 1 - k
                        a = slice(r + 1, BLK)
                        prod = sol_m[:, 0:k * k].rearrange("p (t i) -> p t i", i=k)
                        tt(prod, sol_n[:, r, a].unsqueeze(1).broadcast_to([32, k, k]),
                           sol_t[:, a, a].rearrange("p i t -> p t i"), ALU.mult).then_inc(s["sol_p"], 1)
                        dve.wait_ge(s["sol_p"], j * 15 + k)
                        v.tensor_reduce(sol_t[:, r, a], prod, AX.X, ALU.add).then_inc(s["sol_r"], 1)
                        dve.wait_ge(s["sol_r"], j * 15 + k)

                for t in range(SLOTS):
                    if t == 0:
                        for c in range(AHEAD):
                            split_lo(base + c, c % RING)
                        for w in range(4):
                            dve.wait_ge(tile_out, nt - 3 + w)
                            stt(sh[:, w, :], pq[:, w, 0:T], col(MU + w * CT), qq[:, w, :], ALU.mult, ALU.add
                                ).then_inc(s["shifted"], 1)
                    if t % 2 == 0 and t // 2 + AHEAD < nchunks:
                        split_lo(base + t // 2 + AHEAD, (t // 2 + AHEAD) % RING)
                    if t == 1:
                        dve.wait_ge(s["shifted"], j * 4 + 4)
                        ts(kk, sh[:, 1, :], col(KK), None, ALU.mult).then_inc(s["kk_ok"], 1)
                        dve.wait_ge(s["g_th"], j + 1)
                        stt(s2g, s2g, 1.0, sh[:, 3, :], ALU.add, ALU.mult).then_inc(s["g2_ok"], 1)
                    if t == 2:
                        dve.wait_ge(s["tanh_wa"], j + 1)
                        ts(sga, tanhs, 0.5, 0.5, ALU.mult, ALU.add).then_inc(s["sig_wa"], 1)
                        dve.wait_ge(s["sig_wa"], j + 1)
                        v.tensor_tensor_scan(ls, restart[:], sga[:, 0, :], 0.0, ALU.mult, ALU.add).then_inc(s["cum"], 1)
                        ts(k2, sga[:, 1, :], -1.0, col(KA), ALU.add, ALU.mult).then_inc(s["ka_t"], 1)
                        dve.wait_ge(s["ka_t"], j + 1)
                        stt(k2, k2, 1.0, sh[:, 1, :], ALU.add, ALU.mult).then_inc(s["k2_ok"], 1)
                    if t == 3:
                        dve.wait_ge(s["kk_mm"], j + 1)
                        ts(ksq, B[:, 0:T], 1e-24, None, ALU.max).then_inc(s["kk_max"], 1)
                        dve.wait_ge(s["k2_ok"], j + 1)
                        stt(bon, sh[:, 0, :], col(RK), k2, ALU.mult, ALU.mult).then_inc(s["rk_ok"], 1)
                    if t == 4:
                        dve.wait_ge(s["kk_rt"], j + 1)
                        v.reciprocal(rin, nrm).then_inc(s["kk_rin"], 1)
                    if t == 5:
                        dve.wait_ge(s["exps"], j + 1)
                        tt(kr[:, :, 1, :], sh[:, 0, :].rearrange("p (b t) -> p b t", b=2),
                           gg[:, 0, :].rearrange("p (b t) -> p b t", b=2), ALU.mult)
                        tt(kd, k2, gg[:, 1, :], ALU.mult)
                        dve.wait_ge(s["rk_mm"], j + 1)
                        tt(bon, B[:, T:2 * T], sh[:, 2, :], ALU.mult).then_inc(s["bon_ok"], 1)
                        dve.wait_ge(s["kh_ok"], j + 1)
                        tt(kr[:, :, 0, :], kh.rearrange("p (b t) -> p b t", b=2),
                           gg[:, 2, :].rearrange("p (b t) -> p b t", b=2), ALU.mult)
                        dve.wait_ge(s["bv_ok"], j + 1)
                        stt(bd, bv, -1.0, gg[:, 1, :], ALU.mult, ALU.mult).then_inc(s["prod_ok"], 1)
                    if t == 7:
                        scores(0)
                    if t == 9:
                        scores(1)
                    if t == 13:
                        dve.wait_ge(s["n_in"], j * 16 + 16)
                        solve(1, 9)
                    if t == 14:
                        solve(9, 13)
                    if t == 15:
                        solve(13, 16)
                    if t == 17:
                        dve.wait_ge(s["sc_cx"], j + 1)
                        for k in range(3):
                            if k:
                                dve.wait_ge(s["sc_s"], j * 3 + k)
                                op = stt(scy, scx[:, k:k + T], col(SCW + k * CT), scy, ALU.mult, ALU.add)
                            else:
                                op = ts(scy, scx[:, 0:T], col(SCW), None, ALU.mult)
                            op.then_inc(s["sc_s"], 1)
                        stt(scc, scc, 1.0, scb[:, 3, :], ALU.add, ALU.mult).then_inc(s["sc_g2"], 1)
                        dve.wait_ge(s["sc_s"], j * 3 + 3)
                        stt(scy, scy, 0.5, scb[:, 0, :], ALU.mult, ALU.mult).then_inc(s["sc_b"], 1)
                        dve.wait_ge(s["sc_b"], j + 1)
                        tt(scf, scy, scc, ALU.mult).then_inc(s["sc_f"], 1)
                    if t == 18:
                        dve.wait_ge(s["t_in"], j * 16 + 16)
                        tt(tdt.rearrange("p (q b u) -> p q b u", q=4, b=8),
                           tc[:].unsqueeze(2).broadcast_to([P, 4, 8, BLK]),
                           m16i[:].rearrange("p (b u) -> p b u", b=8).unsqueeze(1).broadcast_to([P, 4, 8, BLK]),
                           ALU.mult).then_inc(s["tdt_ok"], 1)
                    if t == 19:
                        dve.wait_ge(s["oc_hi"], j + 1)
                        tt(olo[:, bass.ds(j, 1), :], scf.unsqueeze(1), ohi[:, bass.ds(j, 1), :].bitcast(F32),
                           ALU.subtract).then_inc(s["oc_ok"], 1)
                    if t == 20:
                        dve.wait_ge(s["ou_mm"], j + 1)
                        tt(xx, A, xx, ALU.add).then_inc(s["xo_ok"], 1)
                    if t == 24:
                        for b in range(2):
                            dve.wait_ge(s["nm_mm"], j * 2 + b + 1)
                            tt(nm[:, b].rearrange("p e c n -> p (e c) n"),
                               ps[:, 6 + b, :].rearrange("p (a n) -> p a n", n=64),
                               ident[:, 64:128].unsqueeze(1).broadcast_to([P, 8, 64]), ALU.add).then_inc(s["nm_ok"], 1)
                    if 25 <= t <= 31:
                        c = t - 25
                        dve.wait_ge(s["gc_ok"], j + 1)
                        dve.wait_ge(s["state_mm"], j * 7 + c + 1)
                        tt(st[64:128, :, c + 1, :], A[64:128, 0:128].rearrange("p (e n) -> p e n", e=2),
                           gcs[64:128, :, c:c + 1].broadcast_to([64, 2, 64]), ALU.mult).then_inc(s["state_ok"], 1)
                    if t == 25:
                        dve.wait_ge(tile_out, nt + 5)
                        conv4(s["x_s"], j * 4, j)
                    if t == 26:
                        dve.wait_ge(s["x_th"], j + 1)
                        stt(xs2, cvt, 1.0, cv, ALU.add, ALU.mult).then_inc(s["xs_ok"], 1)
                        for e in range(2):
                            op = ts(acm[:, e, :], acs[:], ident[0:16, bass.ds(2 * j + e, 1)], None, ALU.mult)
                        op.then_inc(s["acm_ok"], 1)
                        dve.wait_ge(tile_out, nt + 6)
                        stt(zp[:, 1, :], zp[:, 1, :], 1.0, zp[:, 0, :], ALU.add, ALU.mult).then_inc(s["z2_ok"], 1)
                    if t == 27:
                        dve.wait_ge(s["acb_mm"], j + 1)
                        dve.wait_ge(s["dat_ok"], 1)
                        for e in range(2):
                            for b in range(2):
                                op = ts(seg[:, e, b * T:(b * T + T) if b == 0 else 384], E[:, e * T + b * P:e * T + T],
                                        dat[:, 0, b, bass.ds(2 * j + e, 1)], 0.0, ALU.subtract, ALU.min)
                        op.then_inc(s["seg_ok"], 1)
                    if t == 29:
                        dve.wait_ge(s["seg_e"], j + 1)
                        for e in range(2):
                            for b in range(2):
                                r = slice(0, T) if b == 0 else slice(T, 384)
                                op = stt(seg[:, e, r].unsqueeze(1), seg[:, e, r].unsqueeze(1),
                                         dat[:, 1, b, bass.ds(2 * j + e, 1)],
                                         scm[:, bass.ds(j // 2, 1), r], ALU.mult, ALU.mult)
                        op.then_inc(s["seg_g"], 1)
                    if t == 31:
                        dve.wait_ge(s["yb_mm"], j + 1)
                        stt(cv, xs2, dskh[:, bass.ds(j, 1)], C[:, 0:T], ALU.mult, ALU.add).then_inc(s["ob_d"], 1)
                        dve.wait_ge(s["ob_d"], j + 1)
                        stt(o[:, 1, bass.ds(j, 1), :], cv.unsqueeze(1), 0.5, zp[:, 1:2, :], ALU.mult, ALU.mult
                            ).then_inc(s["ob_ok"], 1)
                    if t == 33:
                        dve.wait_ge(s["mean_mm"], j + 1)
                        stt(yc, C[:, 0:T], -1.0 / 64, ys, ALU.mult, ALU.add).then_inc(s["yc_ok"], 1)
                    if t == 36:
                        dve.wait_ge(s["var_rt"], j + 1)
                        v.reciprocal(rin, nrm).then_inc(s["var_r"], 1)
                        dve.wait_ge(s["var_r"], j + 1)
                        tt(yo, yc, rin, ALU.mult).then_inc(s["yn_ok"], 1)
                        dve.wait_ge(s["yn_ok"], j + 1)
                        ts(yo, yo, col(LNW), col(LNB), ALU.mult, ALU.add).then_inc(s["yl_ok"], 1)
                        dve.wait_ge(s["yl_ok"], j + 1)
                        tt(yo, yo, bon, ALU.add).then_inc(s["yb_ok"], 1)
                        dve.wait_ge(s["yb_ok"], j + 1)
                        stt(o[:, 0, bass.ds(j, 1), :], yo.unsqueeze(1), 0.5, s2g.unsqueeze(1), ALU.mult, ALU.mult
                            ).then_inc(s["oa_ok"], 1)

            with dve.Fori(0, CT - 1) as j:
                main(j, False)
            main(CT - 1, True)

            for c in range(AHEAD):
                split_lo(MAIN_END + c, (MAIN_END + c) % RING)
            for n in range(3):
                base = MAIN_END + n * 8 * GATES
                if n > 0:
                    for half in range(2):
                        r = slice(4 * half, 4 * half + 4)
                        dve.wait_ge(s["osp_hi"], 2 * (n - 1) + half + 1)
                        tt(olo[:, r, :], o[:, 2 - n, r, :], ohi[:, r, :].bitcast(F32), ALU.subtract
                           ).then_inc(s["osp_lo"], 1)

                def gates(i, tail):
                    for h in range(2):
                        for q in range(GATES):
                            y = h * GATES + q + AHEAD
                            if not (tail and y >= 2 * GATES):
                                split_lo(base + i * (2 * GATES) + y, (base + y) % RING)
                        for t in range(2):
                            g = 16 * n + i * 4 + 2 * h + t
                            m = merged[:, bass.ds(i * 4 + (2 * h + t), 1), :]
                            dve.wait_ge(tile_out, g + MAIN_TILES + 1)
                            strip = i * 2 + (8 * n + h)
                            if t == 0:
                                dve.wait_ge(y_done, strip + 1)
                            else:
                                dve.wait_ge(chunk_used, strip * GATES + MAIN_END + 6)
                            gate, y_, gy_ = sgt[:, t:t + 1, :], ps[:, t:t + 1, 0:T], gy[:, t:t + 1, :]
                            if n == 0:
                                tt(m, gate, y_, ALU.mult).then_inc(s["gy_ok"], 1)
                            else:
                                tt(gy_, gate, y_, ALU.mult).then_inc(s["gy_ok"], 1)
                                dve.wait_ge(s["gy_ok"], g + 1)
                                tt(m, m, gy_, ALU.add).then_inc(s["mg_ok"], 1)

                if n == 0:
                    gates(0, False)
                    for g in range(4):
                        dve.wait_ge(s["gn_rt"], g + 1)
                        v.reciprocal(sqs[:, 4 + g, :], sqs[:, g, :]).then_inc(s["gn_r"], 1)
                        dve.wait_ge(s["gn_r"], g + 1)
                        for t in range(2):
                            k = 2 * g + t
                            stt(o[:, 1, k, :], o[:, 1, k, :], prm[:, SNW + k:SNW + k + 1], sqs[:, 4 + g, :],
                                ALU.mult, ALU.mult).then_inc(s["gn_ok"], 1)
                with dve.Fori(1 if n == 0 else 0, 3) as i:
                    gates(i, False)
                gates(3, n == 2)
            for k in range(4):
                r = slice(4 * k, 4 * k + 4)
                dve.wait_ge(s["m_hi"], k + 1)
                tt(hlo[:, r, :], merged[:, r, :], hhi[:, r, :].bitcast(F32), ALU.subtract).then_inc(s["m_lo"], 1)
            for k in range(AHEAD):
                split_lo(GATE_END + k, k)
            dve.wait_ge(x_in, 64)

            def outs(i, tail):
                for h in range(2):
                    for q in range(4):
                        y = 4 * h + q + AHEAD
                        if not (tail and y >= 8):
                            split_lo(GATE_END + i * 8 + y, y % RING)
                    for b in range(2):
                        if b == 0:
                            dve.wait_ge(s["out_mm"], i * 2 + (h + 1))
                        else:
                            dve.wait_ge(chunk_used, i * 8 + (GATE_END + 4 * h + 4))
                        r = xtok[:, b, bass.ds(i * (2 * CW) + h * CW, CW)]
                        tt(r, ps[:, 2 * h + b, 0:CW], r, ALU.add).then_inc(s["out_ok"], 1)

            with dve.Fori(0, 3) as i:
                outs(i, False)
            outs(3, True)
            dve.wait_ge(s["f_rt"], 1)
            v.reciprocal(rowst[:, 4:6], rowst[:, 2:4]).then_inc(s["f_rs"], 1)
            dve.wait_ge(s["f_rs"], 1)
            dve.wait_ge(x_in, 80)
            for b in range(2):
                stt(xtok[:, b, :], xtok[:, b, :], rowst[:, 4 + b:5 + b], fnw, ALU.mult, ALU.mult).then_inc(s["f_ok"], 1)

        @block.tensor
        def _(pe):
            mm, tr = nc.tensor.matmul, nc.tensor.transpose

            pe.wait_ge(s["const_z"], 2)
            pe.wait_ge(prm_in, 13 * 16)
            tr(A[:, 0:ROWS0], prow[0:ROWS0, 0, :], ident[0:ROWS0, 0:ROWS0])
            tr(A[:, P:P + ROWS1], prow[0:ROWS1, 1, :], ident[0:ROWS1, 0:ROWS1]).then_inc(s["prm_t"], 1)
            pe.wait_ge(s["x_n"], 2)
            for k in range(KT):
                if k == 0:
                    pe.wait_ge(s["prm_ok"], 1)
                if k >= 4:
                    pe.wait_ge(s["h_lo"], k - 3)
                for b in range(2):
                    op = tr(ps[:, 4 + k % 4, b * P:(b + 1) * P], xtok[:, b, k * P:(k + 1) * P], ident[:])
                op.then_inc(s["x_tr"], 1)
            pe.wait_ge(s["h_lo"], KT)

            def triple(dst, wcol, slot, k, khi, klo, first, last):
                a, b = whi[:, slot, k, wcol], wlo[:, slot, k, wcol]
                mm(dst, a, khi, start=first, stop=False)
                mm(dst, a, klo, start=False, stop=False)
                return mm(dst, b, khi, start=False, stop=last)

            def half_chunk(c, slot, q, t, bank, xh=hhi, xl=hlo, nq=4, width=P, done=tile_done):
                if t == 0:
                    pe.wait_ge(lo_done, c + 1)
                for k in range(KC):
                    kt = q * KC + k
                    op = triple(ps[0:width, bank + t, 0:T], slice(t * P, t * P + width), slot, k, xh[:, kt, :],
                                xl[:, kt, :], kt == 0, kt == nq * KC - 1)
                if q == nq - 1 and t == 0:
                    op.then_inc(done, 1)
                if t == 1:
                    op.then_inc(chunk_used, 1)

            for c in range(PRE):
                strip, q = c // 4, c % 4
                for t in range(2):
                    if q == 0 and strip >= 2:
                        pe.wait_ge(tile_out, 2 * (strip - 2) + t + 1)
                    half_chunk(c, c % RING, q, t, 2 * ((strip + 1) % 2), width=16 if strip == 0 and t == 1 else P)
                if c == 22:
                    for g in range(NG):
                        pe.wait_ge(s["bc_ok"], 8)
                        bg, cg = bc[:, g, :], bc[:, NG + g, :]
                        mm(ps[:, 4 + g, 0:T], bg[:, 0:P], cg, start=True, stop=True)
                        mm(ps[:, 4 + g, T:384], bg[:, P:T], cg[:, P:T], start=True, stop=True).then_inc(s["sc_mm"], 1)
            pe.wait_ge(s["acs_ok"], 1)
            pe.wait_ge(s["scm_ok"], 4)
            for w, src in enumerate((acs[:], dts[:, 5, :])):
                for b in range(2):
                    op = tr(B[:, (2 * w + b) * 16:(2 * w + b + 1) * 16], src[:, b * P:(b + 1) * P], ident[0:16, 0:16])
            op.then_inc(s["dt_tr"], 1)
            pe.wait_ge(s["dat_ok"], 1)
            pe.wait_ge(s["lr_ok"], 1)
            pe.wait_ge(s["const_o"], 1)

            def main(j, last):
                base = PRE + j * ITER
                nt = PRE_TILES + j * ITER_TILES
                free = (nt - 3, nt - 1, nt + 1, nt + 5, nt + 3)

                def score(b):
                    for e in range(2):
                        r = slice(64 * e, 64 * e + 64)
                        c = slice(b * P, b * P + P)
                        dst = ps[:, 4 + e, :]
                        krb = kr[r, b, :, :].rearrange("p w t -> p (w t)")
                        mm(dst[:, 0:T], kd[r, c], krb, start=True, stop=True)
                        mm(dst[:, T:2 * T], bd[r, c], krb, start=True, stop=True).then_inc(s["score_mm"], 1)

                for t in range(SLOTS):
                    if t // 2 < (LAST if last else ITER):
                        c, a = t // 2, t // 8
                        if t % 8 < 2:
                            pe.wait_ge(tile_out, free[a] + t % 2)
                        half_chunk(base + c, c % RING, c % 4, t % 2, BANKS[a])
                    if t == 0:
                        pe.wait_ge(lora_in, j * 32 + 32)
                        mm(A[:, 0:T], lorat[:, 0, :], lr[:], start=True, stop=True)
                        mm(A[:, T:2 * T], lorat[:, 1, :], lr[:], start=True, stop=True).then_inc(s["lora_mm"], 1)
                    if t == 2:
                        pe.wait_ge(s["kk_sq"], j + 1)
                        mm(B[:, 0:T], head1[:], ksq, start=True, stop=True).then_inc(s["kk_mm"], 1)
                    if t == 4:
                        pe.wait_ge(s["kk_max"], j + 1)
                        pe.wait_ge(s["rk_ok"], j + 1)
                        mm(B[:, T:2 * T], head1[:], bon, start=True, stop=True).then_inc(s["rk_mm"], 1)
                    if t == 6:
                        pe.wait_ge(s["prod_ok"], j + 1)
                        pe.wait_ge(s["bon_ok"], j + 1)
                        for dst, one, two, done in ((C, lambda b: sh[:, 2, b * P:(b + 1) * P], lambda b: kr[:, b, 0, :],
                                                     "tr_vk"),
                                                    (E, lambda b: kd[:, b * P:(b + 1) * P],
                                                     lambda b: bd[:, b * P:(b + 1) * P], "tr_kb")):
                            for b in range(2):
                                tr(dst[:, b * T:b * T + P], one(b), ident[:])
                                op = tr(dst[:, b * T + P:b * T + T], two(b), ident[:])
                            op.then_inc(s[done], 1)
                        score(0)
                    if t == 8:
                        pe.wait_ge(s["score_ok"], j * 4 + 2)
                        pe.wait_ge(s["ad_ok"], j * 4 + 2)
                        score(1)
                    if t == 10:
                        pe.wait_ge(s["score_ok"], j * 4 + 4)
                        pe.wait_ge(s["kdbd_ok"], j + 1)
                        for q in range(4):
                            b, e = q // 2, q % 2
                            op = mm(E[:, q * 64:q * 64 + 64], s4[:, q, 0:P], vt[:, b, 64 * e:64 * e + 64],
                                    start=True, stop=True)
                        op.then_inc(s["xv_mm"], 1)
                    if t == 18:
                        pe.wait_ge(s["tdt_ok"], j + 1)
                        pe.wait_ge(s["xv_ok"], j + 1)
                        for q in range(4):
                            r = slice(q * P, q * P + P)
                            op = mm(B[:, r], tdt[:, r], xx[:, r], start=True, stop=True)
                        op.then_inc(s["u_mm"], 1)
                    if t == 19:
                        pe.wait_ge(s["u_ok"], j + 1)
                        for q in range(4):
                            r = slice(q * P, q * P + P)
                            op = mm(A[:, r], s4[:, q, 2 * P:3 * P], uu[:, r], start=True, stop=True)
                        op.then_inc(s["ou_mm"], 1)
                    if t == 20:
                        pe.wait_ge(s["xo_ok"], j + 1)
                        for q in range(4):
                            r = slice(q * P, q * P + P)
                            op = mm(B[:, r], tdt[:, r], xx[:, r], start=True, stop=True)
                        op.then_inc(s["uw_mm"], 1)
                    if t == 21:
                        pe.wait_ge(s["uw_ok"], j + 1)
                        for q in range(4):
                            b, e = q // 2, q % 2
                            r, h = slice(q * P, q * P + P), slice(64 * e, 64 * e + 64)
                            mm(A[:, r], uw[:, q, :], s4[:, q, 3 * P:4 * P], start=True, stop=False, skip_group_check=True)
                            mm(A[0:64, r], vt[:, b, h], s4[:, q, P:2 * P], start=False, stop=True, skip_group_check=True)
                            op = mm(A[64:128, r], ident[:, h], kr[:, b, 1, :], start=False, stop=True,
                                    skip_group_check=True)
                        op.then_inc(s["yz_mm"], 1)
                    if t == 23:
                        for b in range(2):
                            for e in range(2):
                                h = slice(64 * e, 64 * e + 64)
                                dst = ps[:, 6 + b, e * T:e * T + T]
                                mm(dst, uw[:, 2 * b + e, :], kdbd[:, b, 1, :, h], start=True, stop=False,
                                   skip_group_check=True)
                                op = mm(dst[0:64, :], vt[:, b, h], kdbd[:, b, 0, :, h], start=False, stop=True,
                                        skip_group_check=True)
                            op.then_inc(s["nm_mm"], 1)
                        for e in range(2):
                            op = mm(B[64:128, 8 * e:8 * e + 8], ident[:, 64 * e:64 * e + 64], gg[:, 0, 31:T:32],
                                    start=True, stop=True)
                        op.then_inc(s["gc_mm"], 1)
                    if 24 <= t <= 31:
                        c = t - 24
                        b = c // 4
                        if c == 0:
                            pe.wait_ge(s["nm_ok"], j * 2 + 2)
                            pe.wait_ge(s["yz_ok"], j + 1)
                            pe.wait_ge(s["gc_ok"], j + 1)
                        else:
                            pe.wait_ge(s["state_ok"], j * 7 + c)
                        for e in range(2):
                            if c < 7:
                                op = mm(A[64:128, 64 * e:64 * e + 64], nm[:, b, e, c % 4, :], st[:, e, c, :],
                                        start=True, stop=True)
                        if c < 7:
                            op.then_inc(s["state_mm"], 1)
                        for e in range(2):
                            u = slice(32 * (c % 4), 32 * (c % 4) + 32)
                            op = mm(B[64 * e:64 * e + 64, 32 * c:32 * c + 32], st[:, e, c, :], yz[:, 2 * b + e, u],
                                    start=True, stop=True)
                        if c == 7:
                            op.then_inc(s["y_mm"], 1)
                    if t == 26:
                        pe.wait_ge(s["acm_ok"], j + 1)
                        mm(E, ones[0:16, :], acm[:].rearrange("p e t -> p (e t)"), start=True, stop=True
                           ).then_inc(s["acb_mm"], 1)
                        pe.wait_ge(s["xs_ok"], j + 1)
                        for b in range(2):
                            op = tr(C[:, b * P:b * P + P], xs2[:, b * P:b * P + P], ident[:])
                        op.then_inc(s["x_tr2"], 1)
                    if t == 30:
                        pe.wait_ge(s["xst_ok"], j + 1)
                        pe.wait_ge(s["seg_g"], j + 1)
                        for e in range(2):
                            h = slice(64 * e, 64 * e + 64)
                            mm(C[h, 0:T], xst[:, 0, h], seg[:, e, 0:T], start=True, stop=False, skip_group_check=True)
                            op = mm(C[h, P:T], xst[:, 1, h], seg[:, e, T:384], start=False, stop=True,
                                    skip_group_check=True)
                        op.then_inc(s["yb_mm"], 1)
                    if t == 32:
                        pe.wait_ge(s["ys_ok"], j + 1)
                        pe.wait_ge(s["ob_d"], j + 1)
                        mm(C[:, 0:T], head1[:], ys, start=True, stop=True).then_inc(s["mean_mm"], 1)
                    if t == 34:
                        pe.wait_ge(s["ysq_ok"], j + 1)
                        mm(C[:, 0:T], head1[:], ksq, start=True, stop=True).then_inc(s["var_mm"], 1)

            with pe.Fori(0, CT - 1) as j:
                main(j, False)
            main(CT - 1, True)

            for n in range(3):
                base = MAIN_END + n * 8 * GATES

                def gates(i, peeled):
                    for h in range(2):
                        for q in range(GATES):
                            y = h * GATES + q
                            for t in range(2):
                                g = 16 * n + i * 4 + 2 * h + t
                                if q == 0:
                                    pe.wait_ge(tile_out, g + (MAIN_TILES - 1))
                                if q == 4 and not (peeled and h == 0):
                                    pe.wait_ge(s["gy_ok"], g - 1)
                                if q == 4 and peeled and h == 0:
                                    pe.wait_ge(tile_out, MAIN_TILES)
                                    pe.wait_ge(s["oc_ok"], CT)
                                c = base + i * (2 * GATES) + y
                                if q < 4:
                                    half_chunk(c, (base + y) % RING, q, t, 2)
                                else:
                                    half_chunk(c, (base + y) % RING, q - 4, t, 0, ohi, olo, 2, done=y_done)

                if n == 0:
                    gates(0, True)
                    pe.wait_ge(s["sq_ok"], 1)
                    for g in range(4):
                        mm(ps[:, 4 + g, 0:T], ones[:], sqs[:, 2 * g, :], start=True, stop=False)
                        mm(ps[:, 4 + g, 0:T], ones[:], sqs[:, 2 * g + 1, :], start=False, stop=True
                           ).then_inc(s["gn_mm"], 1)
                else:
                    pe.wait_ge(s["osp_lo"], 2 * n)
                with pe.Fori(1 if n == 0 else 0, 4) as i:
                    gates(i, False)

            pe.wait_ge(s["m_lo"], 4)

            def outs(i, peeled):
                for h in range(2):
                    for q in range(4):
                        pe.wait_ge(lo_done, GATE_END + 1 + i * 8 + (4 * h + q))
                        for b in range(2):
                            if q == 0:
                                if peeled:
                                    pe.wait_ge(s["gy_ok"], 48)
                                    pe.wait_ge(tile_out, MAIN_TILES + 48)
                                else:
                                    pe.wait_ge(s["out_ok"], i * 4 + (2 * h + b - 3))
                            for k in range(KC):
                                kt = q * KC + k
                                r = slice(b * P, b * P + P)
                                dst = ps[:, 2 * h + b, 0:CW]
                                mm(dst, hhi[:, kt, r], whi[:, q, k, :], start=kt == 0, stop=False)
                                mm(dst, hhi[:, kt, r], wlo[:, q, k, :], start=False, stop=False)
                                op = mm(dst, hlo[:, kt, r], whi[:, q, k, :], start=False, stop=kt == KT - 1)
                            if q == 3 and b == 0:
                                op.then_inc(s["out_mm"], 1)
                        op.then_inc(chunk_used, 1)

            outs(0, True)
            with pe.Fori(1, 4) as i:
                outs(i, False)


NAMES = ["x", "norm_w", "w_in", "rw_mu", "rw_w0", "rw_w2", "rw_a0", "rw_a2", "rw_kk", "rw_ka", "rw_rk", "rw_ln_w",
         "rw_ln_b", "ssd_conv_w", "ssd_conv_b", "ssd_dt_bias", "ssd_a_log", "ssd_d", "ssd_norm_w", "sc_conv_w",
         "w_branch", "w_out", "final_norm_w"]


def kernel(**inputs):
    import concourse.bacc as bacc
    from concourse.bass_utils import run_bass_kernel_spmd

    nc = bacc.Bacc("TRN2", target_bir_lowering=False, num_devices=1)
    arrays, args = {}, []
    for name in NAMES:
        a = np.ascontiguousarray(inputs[name])
        arrays[f"in_{name}"] = a
        args.append(nc.dram_tensor(f"in_{name}", a.shape, mybir.dt.from_np(a.dtype), kind="ExternalInput").ap())
    args.append(nc.dram_tensor("out_y", (1, T, D), F32, kind="ExternalOutput").ap())
    build_program(nc, *args)
    r = run_bass_kernel_spmd(nc, [arrays], core_ids=[0])
    return r.results[0]["out_y"]
```

```python
from contextlib import ExitStack

import numpy as np
import concourse.bass as bass
from concourse import mybir

F32 = mybir.dt.float32
F32R = mybir.dt.float32r
ALU = mybir.AluOpType
ACT = mybir.ActivationFunctionType
AX = mybir.AxisListType

P = 128
D = 2048
T = 256
W = 1024
KT = D // P
CT = W // P
NG, NS = 4, 128
RW0 = 0
RANKS = 4 * W
SSD0 = RANKS + 128
DT0 = SSD0 + 2 * W + 2 * NG * NS
SC0 = DT0 + 16
GATE0 = SC0 + 4 * W
EXP_M_HALF = float(np.exp(-0.5))
RING = 4
KC = 4
CW = 256
BLK = 16

MU, W0, A0, KK, KA, RK, LNW, LNB, NW, SNW = 0, 33, 41, 49, 57, 65, 73, 81, 89, 105
ROWS0 = 113
CVW, CVB, SCW = 128, 192, 208
ROWS1 = 104

PRE_STRIPS = 7
PRE = PRE_STRIPS * 4
ITER = 20
LAST = 12
MAIN_END = PRE + 7 * ITER + LAST
GATES = 6
GATE_END = MAIN_END + 3 * 8 * GATES
CHUNKS = GATE_END + 8 * 4
PRE_TILES = 2 * PRE_STRIPS
ITER_TILES = 10
LAST_TILES = 6
MAIN_TILES = PRE_TILES + 7 * ITER_TILES + LAST_TILES
SLOTS = 2 * ITER
AHEAD = 2


def build_program(nc, x, norm_w, w_in, rw_mu, rw_w0, rw_w2, rw_a0, rw_a2, rw_kk, rw_ka, rw_rk, rw_ln_w, rw_ln_b,
                  ssd_conv_w, ssd_conv_b, ssd_dt_bias, ssd_a_log, ssd_d, ssd_norm_w, sc_conv_w, w_branch, w_out,
                  final_norm_w, out):
    ctx = ExitStack()
    with ctx:
        def sb(name, shape, dt=F32):
            return ctx.enter_context(nc.sbuf_tensor(name, shape, dt))

        def sem(name):
            return ctx.enter_context(nc.semaphore(name))

        raw = sb("raw", [P, RING, KC, CW])
        whi = sb("whi", [P, RING, KC, CW], F32R)
        wlo = sb("wlo", [P, RING, KC, CW], F32R)
        hhi = sb("hhi", [P, KT, T], F32R)
        hlo = sb("hlo", [P, KT, T], F32R)
        ohi = sb("ohi", [P, CT, T], F32R)
        olo = sb("olo", [P, CT, T], F32R)
        o = sb("o", [P, 2, CT, T])
        xtok = o[:, :, :, :].rearrange("p b j t -> p b (j t)")
        work = sb("work", [P, 4096])
        merged = work[:, :].rearrange("p (k t) -> p k t", k=KT)
        kdbd = work[:, 0:2048].rearrange("p (b w c n) -> p b w c n", b=2, w=2, c=4)
        s4 = work[:, 2048:4096].rearrange("p (q n) -> p q n", q=4)
        bc = work[:, 0:2048].rearrange("p (j t) -> p j t", j=8)

        lots = sb("lots", [P, 44, T])

        def lot(a, n=1):
            return lots[:, a, :] if n == 1 else lots[:, a:a + n, :]

        def flat(a, n):
            return lots[:, a:a + n, :].rearrange("p a t -> p (a t)")

        sh = lot(0, 4)
        gg = lot(4, 2)
        kd = lot(14)
        qq = lot(4, 4)
        bd = lot(8)
        kk, k2, kh, bv = (lot(n) for n in range(9, 13))
        uu = flat(9, 2)
        nm = flat(9, 4).rearrange("p (b e c n) -> p b e c n", b=2, e=2, c=4)
        dts = lots[0:16, 9:15, :]
        ksq, nrm, rin, bon = (lot(n) for n in range(13, 17))
        lshift = lot(15)
        prow = lot(16).rearrange("p (a c) -> p a c", a=2)
        kr = flat(17, 2).rearrange("p (b w t) -> p b w t", b=2, w=2)
        tanhs = lot(19, 2)
        xs2, xst = lot(19), lot(20).rearrange("p (b n) -> p b n", b=2)
        sga, ls, lp = lot(21, 2), lot(23), lot(24)
        seg = flat(21, 3).rearrange("p (e n) -> p e n", e=2)
        uw = flat(23, 2).rearrange("p (q n) -> p q n", q=4)
        vt = lot(25).rearrange("p (b n) -> p b n", b=2)
        xx = flat(26, 2)
        xx5 = xx.rearrange("p (b e w n) -> p b e w n", b=2, e=2, w=2)
        yz = flat(26, 2).rearrange("p (q n) -> p q n", q=4)
        tdt = flat(28, 2)
        ys, yc, ysq = lot(28), lot(29), lot(12)
        rdiag = lot(17).rearrange("p (b t) -> p b t", b=2)
        fnw = flat(32, 8)
        z = flat(0, 16).rearrange("p (b n) -> p b n", b=2)
        knrm, krin = lot(11), lot(10)
        cv, cvt = lot(40), lot(41)
        yo, s2g = lot(30), lot(31)
        sol_n = lots[0:32, 32, :].rearrange("p (s t) -> p s t", s=BLK)
        sol_m = lots[0:32, 33, :]
        sol_t = lots[0:32, 34, :].rearrange("p (s t) -> p s t", s=BLK)
        scb = lot(35, 4)
        scc, scy, scf = lot(39), lot(40), lot(41)
        zp = lot(42, 2)
        sqs = lot(0, 8)
        sgt, gy = lot(21, 2), lot(19, 2)

        prm = sb("prm", [P, 256])
        omm = sb("omm", [P, 33])
        halfb = sb("halfb", [P, 16])
        dsk = sb("dsk", [P, CT])
        dskh = sb("dskh", [P, CT])
        ident = sb("ident", [P, P])
        mask4 = sb("mask4", [P, 4, P])
        m16s = sb("m16s", [P, P])
        m16i = sb("m16i", [P, P])
        head1 = sb("head1", [P, P])
        ones = sb("ones", [P, P])
        causal = sb("causal", [P, 384])
        restart = sb("restart", [P, T])
        eps3 = sb("eps3", [P, 3])
        lorat = sb("lorat", [P, 2, P])
        lr = sb("lr", [P, T])
        rowst = sb("rowst", [P, 24])
        pq = sb("pq", [P, 4, 1 + T])
        adt = sb("adt", [P, P])
        ad = sb("ad", [P, 4, BLK])
        tc = sb("tc", [P, 4, BLK])
        st = sb("st", [P, 2, 8, 64])
        gcs = sb("gcs", [P, 2, 8])
        scx = sb("scx", [P, 2 + T])
        xp = sb("xp", [P, 3 + T])
        scm = sb("scm", [P, NG, 384])
        dtc = sb("dtc", [16, 4])
        acs = sb("acs", [16, T])
        acm = sb("acm", [16, 2, T])
        dat = sb("dat", [P, 2, 2, 16])

        ps = ctx.enter_context(nc.psum_tensor("ps", [P, 8, 512], F32))
        A, B, C, E = (ps[:, n, :] for n in range(4, 8))
        BANKS = (0, 2, 0, 0, 2)

        by_tile = "a (r c) -> (a r) c"
        rows = [(MU, rw_mu.rearrange(by_tile, c=P)), (W0, rw_w0.rearrange(by_tile, c=P)),
                (A0, rw_a0.rearrange(by_tile, c=P)), (KK, rw_kk.rearrange(by_tile, c=P)),
                (KA, rw_ka.rearrange(by_tile, c=P)), (RK, rw_rk.rearrange("a (r e) c -> (a r) (e c)", e=2)),
                (LNW, rw_ln_w.rearrange(by_tile, c=P)), (LNB, rw_ln_b.rearrange(by_tile, c=P)),
                (NW, norm_w.rearrange(by_tile, c=P)), (SNW, ssd_norm_w.rearrange(by_tile, c=P)),
                (CVW, ssd_conv_w.rearrange("a k (r c) -> (a k r) c", c=P)),
                (CVB, ssd_conv_b.rearrange(by_tile, c=P)),
                (SCW, sc_conv_w.rearrange("a k (r c) -> (a k r) c", c=P))]

        x_in, prm_in, lora_in, dtp_in, dsk_in = (sem(n) for n in ("x_in", "prm_in", "lora_in", "dtp_in", "dsk_in"))
        first_x_in = [sem(f"first_x_in{b}") for b in range(2)]
        raw_in = [sem(f"raw_in{n}") for n in range(RING)]
        hi_done, lo_done, chunk_used = sem("hi_done"), sem("lo_done"), sem("chunk_used")
        tile_done, tile_out, y_done = sem("tile_done"), sem("tile_out"), sem("y_done")
        names = """f_sum z_ok kdbd_z const_z const_m const_o prm_t prm_ok prm_d x_sq x_rt x_rs x_n x_tr h_hi h_lo ranks_sh lr_ok
            bc_s bc_th bc_ok sc_mm scm_ok dt_ab dt_e dt_u dt_l dt_d dt_i dt_r dt_c dt_ok dt_ae dt_da acs_ok
            dt_tr dat_ok shifted lora_mm tanh_wa sig_wa cum cum_prev exps kk_ok kk_sq kk_mm kk_max kk_rt kk_rin
            kh_ok ka_t k2_ok rk_ok rk_mm bon_ok bv_ok prod_ok tr_vk tr_kb vt_ok kdbd_ok score_mm score_ok adt_ok
            ad_ok n_in sol_p sol_r t_in tdt_ok xv_mm xv_ok u_mm u_ok ou_mm xo_ok uw_mm uw_ok yz_mm yz_ok nm_mm
            nm_ok gc_mm gc_ok state_mm state_ok y_mm ys_ok mean_mm yc_ok ysq_ok var_mm var_rt var_r yn_ok yl_ok
            yb_ok g_th oa_ok sc_cx sc_s sc_b sc_f oc_hi oc_ok x_s x_th xs_ok z2_ok x_tr2 xst_ok
            acm_ok acb_mm seg_ok seg_e seg_g yb_mm ob_d ob_ok sq_ok gn_mm gn_rt gn_r gn_ok osp_hi osp_lo gy_ok
            mg_ok m_hi m_lo out_mm out_ok f_sq f_act f_rs f_ok stored"""
        s = {n: sem(n) for n in names.split()}

        block = ctx.enter_context(nc.Block())

        @block.sync
        def _(sp):
            for b in range(2):
                sp.dma_start(xtok[:, b, :], x[0, b * P:(b + 1) * P, :]).then_inc(first_x_in[b], 16)

            for r0, src in rows[6:]:
                sp.dma_start(prow[r0 % P:r0 % P + src.shape[0], r0 // P, :], src).then_inc(prm_in, 16)

            def slot_free(c):
                sp.wait_ge(lo_done, c - (RING - 1))

            def strip(c, cols, widths=(P, P), first=False, quarters=range(4)):
                for q in quarters:
                    if not first:
                        slot_free(c + q)
                    for at, c0, w in ((0, cols[0], widths[0]), (P, cols[1], widths[1])):
                        src = w_in[0, q * KC * P:(q + 1) * KC * P, bass.ds(c0, w)].rearrange("(k p) c -> p k c", p=P)
                        sp.dma_start(raw[:, q, :, at:at + w], src).then_inc(raw_in[q], 16)

            def block_chunk(c, slot, src):
                slot_free(c)
                for half in (1, 0):
                    sp.dma_start(raw[:, slot, 2 * half:2 * half + 2, :],
                                 src(half * 2 * P, (half + 1) * 2 * P).rearrange("(k p) c -> p k c", p=P)
                                 ).then_inc(raw_in[slot], 16)

            def load_lora(j):
                sp.dma_start(lorat[0:64, 0, :], rw_w2[0, :, bass.ds(j * P, P)]).then_inc(lora_in, 16)
                sp.dma_start(lorat[64:128, 1, :], rw_a2[0, :, bass.ds(j * P, P)]).then_inc(lora_in, 16)

            strip(0, (RANKS, DT0), (P, 16), first=True)
            sp.dma_start(dtc[:, 0:1], ssd_dt_bias.rearrange("a h -> h a"), allow_slow_non_contiguous=True).then_inc(dtp_in, 16)
            sp.dma_start(dtc[:, 1:2], ssd_a_log.rearrange("a h -> h a"), allow_slow_non_contiguous=True).then_inc(dtp_in, 16)
            by_head = ssd_d.rearrange("a (j e) -> e a j", e=2)
            for e in range(2):
                sp.dma_start(dsk[64 * e:64 * e + 64, :], by_head[e].broadcast_to([64, CT]),
                              allow_slow_non_contiguous=True).then_inc(dsk_in, 16)

            sp.wait_ge(s["const_z"], 2)
            load_lora(0)
            for n in range(4):
                c0 = SSD0 + 2 * W + n * 256
                strip(4 + 4 * n, (c0, c0 + P))
            strip(20, (0, W))
            strip(24, (2 * W, 3 * W))

            def main(j, last):
                c = PRE + j * ITER
                strip(c, (SSD0 + W + j * P, SSD0 + j * P))
                strip(c + 4, (SC0 + j * P, SC0 + W + j * P))
                cols = (SC0 + 2 * W + j * P, SC0 + 3 * W + j * P)
                strip(c + 8, cols, quarters=range(0, 2))
                for q in range(4):
                    sp.wait_ge(s["ad_ok"], j * 4 + q + 1)
                    sp.dma_start(sol_n[8 * q:8 * q + 8, :, :], ad[:, q, :]).then_inc(s["n_in"], 16)
                strip(c + 8, cols, quarters=range(2, 4))
                if not last:
                    cols = ((j + 1) * P, W + (j + 1) * P)
                    strip(c + 12, cols, quarters=range(0, 1))
                sp.wait_ge(s["sol_r"], j * 15 + 15)
                for q in range(4):
                    sp.dma_start(tc[:, q, :], sol_t[8 * q:8 * q + 8, :, :]).then_inc(s["t_in"], 16)
                if not last:
                    strip(c + 12, cols, quarters=range(1, 4))
                    sp.wait_ge(s["lora_mm"], j + 1)
                    load_lora(j + 1)
                    strip(c + 16, (2 * W + (j + 1) * P, 3 * W + (j + 1) * P))

            with sp.Fori(0, CT - 1) as j:
                main(j, False)
            main(CT - 1, True)

            for n in range(3):
                br = 2 - n
                base = MAIN_END + n * 8 * GATES
                with sp.Fori(0, 4) as i:
                    for h in range(2):
                        col = i * (2 * CW) + h * CW
                        for q in range(GATES):
                            if q < 4:
                                def src(a, b):
                                    return w_in[0, q * KC * P + a:q * KC * P + b, bass.ds(col + GATE0 + br * D, CW)]
                            else:
                                def src(a, b):
                                    return w_branch[0, br, (q - 4) * KC * P + a:(q - 4) * KC * P + b, bass.ds(col, CW)]
                            y = h * GATES + q
                            block_chunk(base + i * (2 * GATES) + y, (base + y) % RING, src)
            sp.wait_ge(s["osp_lo"], 4)
            for b in range(2):
                sp.dma_start(xtok[:, b, :], x[0, b * P:(b + 1) * P, :]).then_inc(x_in, 16)
            sp.dma_start(fnw, final_norm_w.rearrange("(a n) -> a n", a=1).broadcast_to([P, D])).then_inc(x_in, 16)
            with sp.Fori(0, 4) as i:
                for h in range(2):
                    for q in range(4):
                        block_chunk(GATE_END + i * 8 + h * 4 + q, q,
                                    lambda a, b: w_out[0, q * KC * P + a:q * KC * P + b, bass.ds(i * (2 * CW) + h * CW, CW)])
            for n, (b, half) in enumerate(((0, 0), (0, 1), (1, 0))):
                sp.wait_ge(s["f_ok"], n + 1)
                sp.dma_start(out[0, b * P:(b + 1) * P, half * 1024:(half + 1) * 1024],
                             z[:, b, half * 1024:(half + 1) * 1024]).then_inc(s["stored"], 16)
            sp.wait_ge(s["stored"], 64)

        @block.gpsimd
        def _(pool):
            gp = nc.gpsimd
            for t, v in ((ident[:], 0.0), (mask4[:], 1.0), (m16s[:], 1.0), (m16i[:], 1.0), (head1[:], 1.0),
                         (ones[:], 1.0), (causal[:], 0.25), (restart[:], 1.0), (st[:], 0.0), (sol_t, 0.0),
                         (lorat[:], 0.0), (pq[:], 0.0), (xp[:], 0.0), (scx[:], 0.0), (eps3[:, 0:1], 1e-6),
                         (eps3[:, 1:2], 64e-5)):
                gp.memset(t, v)
            gp.memset(eps3[:, 2:3], 1e-5).then_inc(s["const_z"], 1)
            pool.wait_ge(s["const_z"], 1)
            gp.affine_select(out=ident[:], in_=ident[:], compare_op=ALU.not_equal, fill=1.0, base=0,
                             pattern=[[-1, P]], channel_multiplier=1)
            gp.affine_select(out=sol_t, in_=sol_t, compare_op=ALU.not_equal, fill=1.0, base=0,
                             pattern=[[1, BLK], [-1, BLK]], channel_multiplier=0)
            for m, base in ((mask4[:, 0, :], -1), (mask4[:, 1, :], 0), (m16s[:], -1), (m16i[:], 0),
                            (causal[:, 0:P], 0), (causal[:, 256:384], 0)):
                gp.affine_select(out=m, in_=m, compare_op=ALU.is_ge, fill=0.0, base=base,
                                 pattern=[[1, P]], channel_multiplier=-1)
            h1 = head1[:].rearrange("p (e u) -> p e u", e=2)
            gp.affine_select(out=h1, in_=h1, compare_op=ALU.is_ge, fill=0.0, base=0,
                             pattern=[[-64, 2], [0, 64]], channel_multiplier=1).then_inc(s["const_z"], 1)
            pool.wait_ge(s["const_z"], 2)
            for m, n in ((mask4[:, 0, :], 4), (mask4[:, 1, :], 4), (m16s[:], 8), (m16i[:], 8)):
                v = m.rearrange("p (b u) -> p b u", b=n)
                gp.affine_select(out=v, in_=v, compare_op=ALU.is_ge, fill=0.0, base=0,
                                 pattern=[[-(P // n), n], [0, P // n]], channel_multiplier=1)
            gp.affine_select(out=h1, in_=h1, compare_op=ALU.is_ge, fill=0.0, base=63,
                             pattern=[[64, 2], [0, 64]], channel_multiplier=-1)
            gp.memset(restart[:].rearrange("p (c u) -> p c u", u=32)[:, :, 0:1], 0.0).then_inc(s["const_m"], 1)

            def kk_square(j):
                pool.wait_ge(s["kk_ok"], j + 1)
                gp.tensor_tensor(ksq, kk, kk, ALU.mult).then_inc(s["kk_sq"], 1)

            def kk_unit(j):
                pool.wait_ge(s["kk_rin"], j + 1)
                gp.tensor_tensor(kh, kk, krin, ALU.mult).then_inc(s["kh_ok"], 1)
                pool.wait_ge(s["cum"], j + 1)
                gp.tensor_tensor(lp, ls, sga[:, 0, :], ALU.subtract).then_inc(s["cum_prev"], 1)

            def main(j, last):
                pool.wait_ge(s["kh_ok"], j + 1)
                gp.tensor_tensor(bv, kh, sga[:, 1, :], ALU.mult).then_inc(s["bv_ok"], 1)
                pool.wait_ge(tile_out, j * ITER_TILES + PRE_TILES + 6)
                gp.tensor_tensor(scx[:, 2:2 + T], scb[:, 1, :], scb[:, 2, :], ALU.mult).then_inc(s["sc_cx"], 1)
                pool.wait_ge(s["yc_ok"], j + 1)
                gp.tensor_tensor(ysq, yc, yc, ALU.mult).then_inc(s["ysq_ok"], 1)
                if not last:
                    kk_square(j + 1)
                    kk_unit(j + 1)

            pool.wait_ge(s["sc_mm"], NG)
            gp.memset(kdbd, 0.0).then_inc(s["kdbd_z"], 1)

            kk_square(0)
            kk_unit(0)
            with gp.Fori(0, CT - 1) as j:
                main(j, False)
            main(CT - 1, True)
            pool.wait_ge(s["ob_ok"], CT)
            pool.wait_ge(s["oa_ok"], CT)
            for j in range(CT):
                last = gp.tensor_tensor(sqs[:, j, :], o[:, 1, j, :], o[:, 1, j, :], ALU.mult)
            last.then_inc(s["sq_ok"], 1)

        @block.scalar
        def _(act):
            sc = nc.scalar
            for r0, src in rows[:6]:
                act.dma_start(prow[r0 % P:r0 % P + src.shape[0], r0 // P, :], src).then_inc(prm_in, 16)
            act.wait_ge(s["const_z"], 1)
            sc.activation(rowst[:, 6:7], eps3[:, 0:1], ACT.Sqrt)
            for b in range(2):
                act.wait_ge(first_x_in[b], 16)
                sc.activation(work[:, b * D:(b + 1) * D], xtok[:, b, :], ACT.Square,
                              accum_out=rowst[:, b:b + 1]).then_inc(s["x_sq"], 1)
            act.wait_ge(s["const_z"], 2)
            act.wait_ge(s["x_sq"], 2)
            sc.activation(rowst[:, 2:4], rowst[:, 0:2], ACT.Sqrt, scale=1.0 / D, bias=eps3[:, 0:1]).then_inc(s["x_rt"], 1)
            act.wait_ge(s["prm_t"], 1)
            sc.activation(prm[:, 0:ROWS0], A[:, 0:ROWS0], ACT.Copy)
            sc.activation(prm[:, P:P + ROWS1], A[:, P:P + ROWS1], ACT.Copy).then_inc(s["prm_ok"], 1)
            act.wait_ge(s["prm_ok"], 1)
            def split_hi(c, slot, use, width=CW, first=False):
                act.wait_ge(raw_in[slot], use * 32)
                if not first:
                    act.wait_ge(chunk_used, c - (RING - 1))
                sc.activation(whi[:, slot, :, 0:width], raw[:, slot, :, 0:width], ACT.Copy).then_inc(hi_done, 1)

            def proj(strip, t, bank, dst):
                if t == 0:
                    act.wait_ge(tile_done, strip + 1)
                else:
                    act.wait_ge(chunk_used, strip * 4 + 4)
                return sc.activation(dst, ps[:, bank, 0:T], ACT.Copy)

            def shift_pair(j, a, bank, strip):
                for t in range(2):
                    w = 2 * a + t
                    proj(strip, t, bank + t, pq[:, w, 1:1 + T])
                    sc.activation(qq[:, w, :], ps[:, bank + t, 0:T], ACT.Copy,
                                  scale=omm[:, bass.ds(j + w * CT, 1)]).then_inc(tile_out, 1)

            for k in range(KT):
                act.wait_ge(s["x_tr"], k + 1)
                sc.activation(hhi[:, k, :], ps[:, 4 + k % 4, 0:T], ACT.Copy,
                              scale=prm[:, NW + k:NW + k + 1]).then_inc(s["h_hi"], 1)
                if k in (3, 7, 11):
                    split_hi(k // 4, k // 4, 1, P + 16, first=True)
            act.wait_ge(s["prm_d"], 1)
            for c in range(PRE):
                n = c + AHEAD
                if n > 2:
                    split_hi(n, n % RING, n // RING + 1, P + 16 if n < 4 else CW, first=n < RING)
                if c == 4:
                    act.wait_ge(s["const_m"], 1)
                    proj(0, 0, 2, pq[:, 0, 1:1 + T])
                    sc.activation(qq[:, 0, :], ps[:, 2, 0:T], ACT.Copy, scale=omm[:, 32:33]).then_inc(tile_out, 1)
                    act.wait_ge(chunk_used, 4)
                    act.wait_ge(dtp_in, 32)
                    sc.activation(dts[:, 0, :], ps[0:16, 3, 0:T], ACT.Identity, bias=dtc[:, 0:1]).then_inc(tile_out, 1)
                if c % 4 == 0 and 8 <= c <= 20:
                    for t in range(2):
                        m = 2 * (c // 4 - 2) + t
                        if m >= 1:
                            act.wait_ge(s["bc_s"], 4 * m)
                        proj(c // 4 - 1, t, 2 * ((c // 4) % 2) + t, xp[:, 3:3 + T]).then_inc(tile_out, 1)
                        act.wait_ge(s["bc_s"], 4 * m + 4)
                        sc.activation(cvt, cv, ACT.Tanh, scale=0.5).then_inc(s["bc_th"], 1)
                if c == 24:
                    act.wait_ge(s["ranks_sh"], 1)
                    sc.activation(lr[0:64, :], lshift[0:64, :], ACT.Tanh)
                    sc.activation(lr[64:128, :], lshift[64:128, :], ACT.Copy).then_inc(s["lr_ok"], 1)
                    act.wait_ge(s["dt_ab"], 1)
                    sc.activation(dts[:, 2, :], dts[:, 1, :], ACT.Exp, scale=-1.0).then_inc(s["dt_e"], 1)
                    sc.activation(dtc[:, 2:3], dtc[:, 1:2], ACT.Exp).then_inc(s["dt_ae"], 1)
                    act.wait_ge(s["dt_u"], 1)
                    sc.activation(dts[:, 4, :], dts[:, 3, :], ACT.Ln).then_inc(s["dt_l"], 1)
                    shift_pair(0, 0, 0, 5)
            act.wait_ge(s["dt_tr"], 1)
            sc.activation(dat[:].rearrange("p w b h -> p (w b h)"), B[:, 0:64], ACT.Copy).then_inc(s["dat_ok"], 1)

            def kk_root(j):
                act.wait_ge(s["kk_max"], j + 1)
                sc.activation(knrm, ksq, ACT.Sqrt).then_inc(s["kk_rt"], 1)

            def half_logits(j):
                act.wait_ge(s["lora_mm"], j + 1)
                sc.activation(tanhs[:, 0, :], A[:, 0:T], ACT.Tanh, scale=0.5, bias=halfb[:, bass.ds(j, 1)])
                sc.activation(tanhs[:, 1, :], A[:, T:2 * T], ACT.Tanh, scale=0.5,
                              bias=halfb[:, bass.ds(j + CT, 1)]).then_inc(s["tanh_wa"], 1)

            def gate_split(n, i, y):
                base = MAIN_END + n * 8 * GATES
                split_hi(base + i * (2 * GATES) + y, (base + y) % RING, (base + y) // RING + 1 + i * (2 * GATES // RING))

            def sigmoids(n, i, h, first=False):
                for t in range(2):
                    g = 16 * n + i * 4 + 2 * h + t
                    strip = i * 2 + (8 * n + h)
                    if t == 0:
                        act.wait_ge(tile_done, strip + MAIN_TILES // 2 + 1)
                    else:
                        act.wait_ge(chunk_used, strip * GATES + MAIN_END + 4)
                    if not first:
                        act.wait_ge(s["gy_ok"], g - 1)
                    sc.activation(sgt[:, t, :], ps[:, 2 + t, 0:T], ACT.Sigmoid).then_inc(tile_out, 1)

            kk_root(0)
            half_logits(0)

            def main(j, last):
                base = PRE + j * ITER
                strip0 = PRE_STRIPS + j * 5
                nchunks = LAST if last else ITER

                def split(c):
                    split_hi(base + c, c % RING, PRE // RING + j * (ITER // RING) + c // RING + 1)

                for t in range(2 * (LAST + 2 * GATES) if last else SLOTS):
                    if t % 2 == 0 and t // 2 < nchunks:
                        split(t // 2 + AHEAD)
                    if t >= 2 * nchunks:
                        h, q = divmod(t // 2 - nchunks, GATES)
                        if t % 2 == 0:
                            gate_split(0, 0, h * GATES + q + AHEAD)
                        elif q == 4:
                            sigmoids(0, 0, h, first=h == 0)
                    if t == 0:
                        act.wait_ge(s["cum"], j + 1)
                        sc.activation(gg[:, 0, :], ls, ACT.Exp, scale=-EXP_M_HALF)
                        sc.activation(gg[:, 1, :], ls, ACT.Exp, scale=EXP_M_HALF)
                        act.wait_ge(s["cum_prev"], j + 1)
                        sc.activation(lp, lp, ACT.Exp, scale=-EXP_M_HALF).then_inc(s["exps"], 1)
                        shift_pair(j, 1, BANKS[4], strip0 - 1)
                    if t == 21:
                        act.wait_ge(s["shifted"], j * 4 + 4)
                        sc.activation(s2g, sh[:, 3, :], ACT.Tanh, scale=0.5).then_inc(s["g_th"], 1)
                    if t == 4:
                        act.wait_ge(s["acs_ok"], 1)
                        for e in range(2):
                            op = sc.activation(acm[:, e, :], acs[:], ACT.Copy, scale=ident[0:16, bass.ds(2 * j + e, 1)])
                        op.then_inc(s["acm_ok"], 1)
                    if t == 5:
                        act.wait_ge(s["tr_vk"], j + 1)
                        cvk = C.rearrange("p (b w n) -> p b w n", b=2, w=2)
                        sc.activation(vt, cvk[:, :, 0, :], ACT.Copy)
                        sc.activation(xx5[:, :, :, 1, :], cvk[:, :, 1, :].rearrange("p b (e n) -> p b e n", e=2),
                                      ACT.Copy).then_inc(s["vt_ok"], 1)
                        act.wait_ge(s["tr_kb"], j + 1)
                        act.wait_ge(s["kdbd_z"], 1)
                        dkb = E.rearrange("p (b w n) -> p b w n", b=2, w=2)
                        for c in range(4):
                            r = slice(32 * c, 32 * c + 32)
                            op = sc.activation(kdbd[r, :, :, c, :], dkb[r, :, :, :], ACT.Copy)
                        op.then_inc(s["kdbd_ok"], 1)
                    if t == 8:
                        proj(strip0, 0, BANKS[0], xp[:, 3:3 + T]).then_inc(tile_out, 1)
                        proj(strip0, 1, BANKS[0] + 1, zp[:, 0, :])
                        sc.activation(zp[:, 1, :], ps[:, BANKS[0] + 1, 0:T], ACT.Tanh, scale=0.5).then_inc(tile_out, 1)
                    if t == 10:
                        act.wait_ge(s["x_s"], j * 4 + 4)
                        sc.activation(cvt, cv, ACT.Tanh, scale=0.5).then_inc(s["x_th"], 1)
                    if t == 10:
                        act.wait_ge(s["acb_mm"], j + 1)
                        for e in range(2):
                            for b in range(2):
                                op = sc.activation(seg[:, e, b * T:(b * T + T) if b == 0 else 384],
                                                   A[:, e * T + b * P:e * T + T], ACT.Relu, scale=-1.0,
                                                   bias=dat[:, 0, b, bass.ds(2 * j + e, 1)])
                        op.then_inc(s["seg_ok"], 1)
                        act.wait_ge(s["seg_ok"], j + 1)
                        sc.activation(seg, seg, ACT.Exp, scale=-1.0).then_inc(s["seg_e"], 1)
                    if t == 12:
                        act.wait_ge(s["xv_mm"], j + 1)
                        sc.activation(xx5[:, :, :, 0, :], E[:, 0:T].rearrange("p (b e n) -> p b e n", b=2, e=2),
                                      ACT.Copy).then_inc(s["xv_ok"], 1)
                    if t == 14:
                        act.wait_ge(s["x_tr2"], j + 1)
                        sc.activation(xst.rearrange("p b n -> p (b n)"), C[:, 0:T], ACT.Copy,
                                      scale=0.5).then_inc(s["xst_ok"], 1)
                    if t == 16:
                        proj(strip0 + 1, 0, BANKS[1], scb[:, 0, :]).then_inc(tile_out, 1)
                        proj(strip0 + 1, 1, BANKS[1] + 1, scb[:, 1, :]).then_inc(tile_out, 1)
                    if t == 20:
                        act.wait_ge(s["u_mm"], j + 1)
                        sc.activation(uu, B, ACT.Copy).then_inc(s["u_ok"], 1)
                    if t == 22:
                        act.wait_ge(s["uw_mm"], j + 1)
                        sc.activation(uw.rearrange("p q n -> p (q n)"), B, ACT.Copy).then_inc(s["uw_ok"], 1)
                    if t == 24:
                        act.wait_ge(s["gc_mm"], j + 1)
                        sc.activation(gcs[64:128, :, :], B[64:128, 0:16].rearrange("p (e c) -> p e c", e=2),
                                      ACT.Copy).then_inc(s["gc_ok"], 1)
                    if t == 24:
                        proj(strip0 + 2, 0, BANKS[2], scb[:, 2, :]).then_inc(tile_out, 1)
                        proj(strip0 + 2, 1, BANKS[2] + 1, scb[:, 3, :])
                        sc.activation(scc, ps[:, BANKS[2] + 1, 0:T], ACT.Tanh, scale=0.5).then_inc(tile_out, 1)
                    if t == 23:
                        act.wait_ge(s["yz_mm"], j + 1)
                        sc.activation(yz.rearrange("p q n -> p (q n)"), A, ACT.Copy).then_inc(s["yz_ok"], 1)
                    if t == 30:
                        act.wait_ge(s["sc_f"], j + 1)
                        sc.activation(ohi[:, bass.ds(j, 1), :], scf.unsqueeze(1), ACT.Copy).then_inc(s["oc_hi"], 1)
                    if t == 32:
                        act.wait_ge(s["y_mm"], j + 1)
                        sc.activation(ys, B[:, 0:T], ACT.Copy).then_inc(s["ys_ok"], 1)
                    if t == 32 and not last:
                        shift_pair(j + 1, 0, BANKS[3], strip0 + 3)
                    if t == 35:
                        act.wait_ge(s["var_mm"], j + 1)
                        sc.activation(nrm, C[:, 0:T], ACT.Sqrt, scale=1.0 / 64, bias=eps3[:, 1:2]).then_inc(s["var_rt"], 1)
                    if t == 36 and not last:
                        kk_root(j + 1)
                    if t == 38 and not last:
                        half_logits(j + 1)

            with act.Fori(0, CT - 1) as j:
                main(j, False)
            main(CT - 1, True)

            def split_merged(k):
                sc.activation(hhi[:, 4 * k:4 * k + 4, :], merged[:, 4 * k:4 * k + 4, :], ACT.Copy).then_inc(s["m_hi"], 1)

            for n in range(3):
                if n > 0:
                    base = MAIN_END + n * 8 * GATES
                    act.wait_ge(s["gn_ok"] if n == 1 else s["oa_ok"], CT)
                    act.wait_ge(chunk_used, base)
                    for half in range(2):
                        r = slice(4 * half, 4 * half + 4)
                        sc.activation(ohi[:, r, :], o[:, 2 - n, r, :], ACT.Copy).then_inc(s["osp_hi"], 1)

                def gates(i, tail=False, group_norm=False):
                    for h in range(2):
                        for q in range(GATES):
                            gate_split(n, i, h * GATES + q + AHEAD)
                            if q == 4:
                                sigmoids(n, i, h)
                            if group_norm and h * GATES + q == 6:
                                for g in range(4):
                                    act.wait_ge(s["gn_mm"], g + 1)
                                    sc.activation(sqs[:, g, :], ps[:, 4 + g, 0:T], ACT.Sqrt, scale=1.0 / 256,
                                                  bias=eps3[:, 2:3]).then_inc(s["gn_rt"], 1)
                    if tail:
                        act.wait_ge(chunk_used, GATE_END - 2)
                        act.wait_ge(s["mg_ok"], 28)
                        for k in range(3):
                            split_merged(k)

                if n == 0:
                    gates(1, group_norm=True)
                with act.Fori(2 if n == 0 else 0, 3) as i:
                    gates(i)
                gates(3, tail=n == 2)
            split_hi(GATE_END + 2, 2, GATE_END // RING + 1)
            act.wait_ge(s["mg_ok"], 32)
            split_merged(3)

            def outs(i, tail):
                for h in range(2):
                    for q in range(4):
                        y = 4 * h + q + AHEAD + 1
                        if not (tail and y >= 8):
                            split_hi(GATE_END + i * 8 + y, y % RING, GATE_END // RING + 1 + i * 2 + y // RING)
                    for b in range(2):
                        act.wait_ge(s["out_ok"], i * 4 + (2 * h + b + 1))
                        sc.activation(lots[:, bass.ds(i * 2 + (16 + 8 * b + h), 1), :],
                                      xtok[:, b:b + 1, bass.ds(i * (2 * CW) + h * CW, CW)], ACT.Square,
                                      accum_out=rowst[:, bass.ds(i * 2 + (8 + 8 * b + h), 1)]).then_inc(s["f_sq"], 1)

            with act.Fori(0, 3) as i:
                outs(i, False)
            sc.activation(rowst[:, 6:7], eps3[:, 0:1], ACT.Sqrt)
            outs(3, True)
            act.wait_ge(s["f_sum"], 1)
            sc.activation(rowst[:, 2:4], rowst[:, 0:2], ACT.Sqrt, scale=1.0 / D, bias=eps3[:, 0:1]).then_inc(s["f_act"], 1)
            act.wait_ge(s["f_rs"], 1)
            act.wait_ge(s["z_ok"], 16)
            sc.activation(z[:, 1, 1024:D], z[:, 1, 1024:D], ACT.Copy, scale=rowst[:, 5:6]).then_inc(s["f_act"], 1)
            act.wait_ge(s["f_act"], 2)
            act.dma_start(out[0, P:2 * P, 1024:D], z[:, 1, 1024:D]).then_inc(s["stored"], 16)

        @block.vector
        def _(dve):
            v = nc.vector
            tt, ts, stt = v.tensor_tensor, v.tensor_scalar, v.scalar_tensor_tensor

            dve.wait_ge(s["const_m"], 1)
            v.tensor_copy(st[0:64, :, :, :].rearrange("p e c n -> p (e c) n"),
                          ident[0:64, 0:64].unsqueeze(1).broadcast_to([64, 16, 64]))
            v.tensor_copy(mask4[:, 3, :], mask4[:, 1, :])
            tt(mask4[:, 2, :], mask4[:, 0, :], m16s[:], ALU.subtract).then_inc(s["const_o"], 1)
            dve.wait_ge(s["x_rt"], 1)
            v.reciprocal(rowst[:, 4:6], rowst[:, 2:4]).then_inc(s["x_rs"], 1)
            dve.wait_ge(s["x_rs"], 1)
            for b in range(2):
                ts(rdiag[:, b, :], ident[:], rowst[:, 4 + b:5 + b], None, ALU.mult).then_inc(s["x_n"], 1)
            dve.wait_ge(s["prm_ok"], 1)
            ts(omm[:], prm[:, MU:MU + 33], -1.0, 1.0, ALU.mult, ALU.add)
            ts(halfb[:], prm[:, W0:W0 + 16], 0.5, None, ALU.mult)
            def split_lo(c, slot, width=CW):
                dve.wait_ge(hi_done, c + 1)
                tt(wlo[:, slot, :, 0:width], raw[:, slot, :, 0:width], whi[:, slot, :, 0:width].bitcast(F32),
                   ALU.subtract).then_inc(lo_done, 1)

            def conv_tap(done, at, ch, k):
                tap = prm[:, bass.ds(ch + (CVW + 16 * k), 1)]
                if k:
                    dve.wait_ge(done, at + k)
                    op = stt(cv, xp[:, k:k + T], tap, cv, ALU.mult, ALU.add)
                else:
                    op = ts(cv, xp[:, 0:T], tap, prm[:, bass.ds(ch + CVB, 1)], ALU.mult, ALU.add)
                op.then_inc(done, 1)

            def conv4(done, at, ch):
                for k in range(4):
                    conv_tap(done, at, ch, k)

            for k in range(KT):
                dve.wait_ge(s["h_hi"], k + 1)
                stt(hlo[:, k, :], ps[:, 4 + k % 4, 0:T], prm[:, NW + k:NW + k + 1], hhi[:, k, :].bitcast(F32),
                    ALU.mult, ALU.subtract).then_inc(s["h_lo"], 1)
                if k in (3, 7, 11):
                    split_lo(k // 4, k // 4, P + 16)
            dve.wait_ge(dsk_in, 32)
            ts(dskh[:], dsk[:], 0.5, None, ALU.mult).then_inc(s["prm_d"], 1)
            for c in range(PRE):
                n = c + AHEAD
                if n > 2:
                    split_lo(n, n % RING, P + 16 if n < 4 else CW)
                if c == 4:
                    dve.wait_ge(tile_out, 1)
                    stt(lshift, pq[:, 0, 0:T], prm[:, MU + 32:MU + 33], qq[:, 0, :], ALU.mult, ALU.add
                        ).then_inc(s["ranks_sh"], 1)
                    dve.wait_ge(tile_out, 2)
                    stt(dts[:, 1, :], dts[:, 0, :], -1.0, dts[:, 0, :], ALU.mult, ALU.max).then_inc(s["dt_ab"], 1)
                if c % 4 == 0 and 8 <= c <= 20:
                    for t in range(2):
                        m = 2 * (c // 4 - 2) + t
                        dve.wait_ge(tile_out, 3 + m)
                        conv4(s["bc_s"], 4 * m, 8 + m)
                        dve.wait_ge(s["bc_th"], m + 1)
                        stt(bc[:, m, :], cvt, 1.0, cv, ALU.add, ALU.mult).then_inc(s["bc_ok"], 1)
                        dve.wait_ge(s["bc_ok"], m + 1)
                if c == 24:
                    dve.wait_ge(s["dt_e"], 1)
                    ts(dts[:, 3, :], dts[:, 2, :], 1.0, None, ALU.add).then_inc(s["dt_u"], 1)
                    dve.wait_ge(s["dt_u"], 1)
                    stt(dts[:, 1, :], dts[:, 3, :], -1.0, dts[:, 2, :], ALU.add, ALU.subtract).then_inc(s["dt_d"], 1)
                    v.reciprocal(dts[:, 5, :], dts[:, 3, :]).then_inc(s["dt_i"], 1)
                    dve.wait_ge(s["dt_i"], 1)
                    dve.wait_ge(s["dt_d"], 1)
                    tt(dts[:, 2, :], dts[:, 1, :], dts[:, 5, :], ALU.mult).then_inc(s["dt_r"], 1)
                    dve.wait_ge(s["dt_r"], 1)
                    dve.wait_ge(s["dt_l"], 1)
                    tt(dts[:, 1, :], dts[:, 4, :], dts[:, 2, :], ALU.subtract).then_inc(s["dt_c"], 1)
                    dve.wait_ge(s["dt_c"], 1)
                    stt(dts[:, 5, :], dts[:, 0, :], 0.0, dts[:, 1, :], ALU.max, ALU.add).then_inc(s["dt_ok"], 1)
                    dve.wait_ge(s["dt_ok"], 1)
                    dve.wait_ge(s["dt_ae"], 1)
                    ts(dts[:, 3, :], dts[:, 5, :], dtc[:, 2:3], -1.0, ALU.mult, ALU.mult).then_inc(s["dt_da"], 1)
                    dve.wait_ge(s["dt_da"], 1)
                    v.tensor_tensor_scan(acs[:], ones[0:16, 0:1].broadcast_to([16, T]), dts[:, 3, :], 0.0,
                                         ALU.mult, ALU.add).then_inc(s["acs_ok"], 1)
                    for g in range(NG):
                        dve.wait_ge(s["sc_mm"], g + 1)
                        tt(scm[:, g, :], ps[:, 4 + g, 0:384], causal[:], ALU.mult).then_inc(s["scm_ok"], 1)

            def shift(j, w):
                dve.wait_ge(tile_out, PRE_TILES + j * ITER_TILES - 3 + w)
                stt(sh[:, w, :], pq[:, w, 0:T], prm[:, bass.ds(j + (MU + w * CT), 1)], qq[:, w, :], ALU.mult, ALU.add
                    ).then_inc(s["shifted"], 1)

            def shift_rk(j):
                shift(j, 1)
                dve.wait_ge(s["shifted"], j * 4 + 1)
                ts(kk, sh[:, 1, :], prm[:, bass.ds(j + KK, 1)], None, ALU.mult).then_inc(s["kk_ok"], 1)
                shift(j, 0)

            def kk_floor(j):
                dve.wait_ge(s["kk_mm"], j + 1)
                ts(ksq, B[:, 0:T], 1e-24, None, ALU.max).then_inc(s["kk_max"], 1)

            def kk_recip(j):
                dve.wait_ge(s["kk_rt"], j + 1)
                v.reciprocal(krin, knrm).then_inc(s["kk_rin"], 1)

            def decays(j):
                dve.wait_ge(s["tanh_wa"], j + 1)
                ts(sga, tanhs, 0.5, 0.5, ALU.mult, ALU.add).then_inc(s["sig_wa"], 1)
                dve.wait_ge(s["sig_wa"], j + 1)
                v.tensor_tensor_scan(ls, restart[:], sga[:, 0, :], 0.0, ALU.mult, ALU.add).then_inc(s["cum"], 1)

            def gate_split(n, i, y):
                base = MAIN_END + n * 8 * GATES
                split_lo(base + i * (2 * GATES) + y, (base + y) % RING)

            def gated(n, i, h):
                for t in range(2):
                    g = 16 * n + i * 4 + 2 * h + t
                    m = merged[:, bass.ds(i * 4 + (2 * h + t), 1), :]
                    dve.wait_ge(tile_out, g + MAIN_TILES + 1)
                    strip = i * 2 + (8 * n + h)
                    if t == 0:
                        dve.wait_ge(y_done, strip + 1)
                    else:
                        dve.wait_ge(chunk_used, strip * GATES + MAIN_END + 6)
                    gate, y_, gy_ = sgt[:, t:t + 1, :], ps[:, t:t + 1, 0:T], gy[:, t:t + 1, :]
                    if n == 0:
                        tt(m, gate, y_, ALU.mult).then_inc(s["gy_ok"], 1)
                    else:
                        tt(gy_, gate, y_, ALU.mult).then_inc(s["gy_ok"], 1)
                        dve.wait_ge(s["gy_ok"], g + 1)
                        tt(m, m, gy_, ALU.add).then_inc(s["mg_ok"], 1)

            shift_rk(0)
            kk_floor(0)
            kk_recip(0)
            decays(0)

            def main(j, last):
                base = PRE + j * ITER
                nt = PRE_TILES + j * ITER_TILES
                nchunks = LAST if last else ITER

                def col(at):
                    return prm[:, bass.ds(j + at, 1)]

                def scores(b):
                    for e in range(2):
                        q = 2 * b + e
                        dve.wait_ge(s["score_mm"], j * 4 + q + 1)
                        src = ps[:, 4 + e, :]
                        tt(adt[:], src[:, 256:384], m16s[:], ALU.mult).then_inc(s["adt_ok"], 1)
                        tt(s4[:, q, :], src, mask4[:].rearrange("p a t -> p (a t)"), ALU.mult).then_inc(s["score_ok"], 1)
                        dve.wait_ge(s["adt_ok"], j * 4 + q + 1)
                        v.tensor_reduce(ad[:, q, :], adt[:].rearrange("p (b u) -> p u b", u=BLK), AX.X, ALU.add
                                        ).then_inc(s["ad_ok"], 1)
                        dve.wait_ge(s["ad_ok"], j * 4 + q + 1)

                def solve_step(k):
                    r = BLK - 1 - k
                    a = slice(r + 1, BLK)
                    prod = sol_m[:, 0:k * k].rearrange("p (t i) -> p t i", i=k)
                    if k > 1:
                        dve.wait_ge(s["sol_r"], j * 15 + k - 1)
                    tt(prod, sol_n[:, r, a].unsqueeze(1).broadcast_to([32, k, k]),
                       sol_t[:, a, a].rearrange("p i t -> p t i"), ALU.mult).then_inc(s["sol_p"], 1)
                    dve.wait_ge(s["sol_p"], j * 15 + k)
                    v.tensor_reduce(sol_t[:, r, a], prod, AX.X, ALU.add).then_inc(s["sol_r"], 1)

                def seg_times(e, b):
                    r = slice(0, T) if b == 0 else slice(T, 384)
                    return stt(seg[:, e, r].unsqueeze(1), seg[:, e, r].unsqueeze(1),
                               dat[:, 1, b, bass.ds(2 * j + e, 1)],
                               scm[:, bass.ds(j // 2, 1), r], ALU.mult, ALU.mult)

                for t in range(2 * (LAST + 2 * GATES) if last else SLOTS):
                    if t % 2 == 0 and t // 2 < nchunks:
                        split_lo(base + t // 2 + AHEAD, (t // 2 + AHEAD) % RING)
                    if t >= 2 * nchunks and t % 2 == 0:
                        gate_split(0, 0, t // 2 - nchunks + AHEAD)
                        if t == 2 * (nchunks + GATES):
                            gated(0, 0, 0)
                    if t == 0:
                        dve.wait_ge(s["kh_ok"], j + 1)
                        ts(k2, sga[:, 1, :], -1.0, col(KA), ALU.add, ALU.mult).then_inc(s["ka_t"], 1)
                        dve.wait_ge(s["ka_t"], j + 1)
                        stt(k2, k2, 1.0, sh[:, 1, :], ALU.add, ALU.mult).then_inc(s["k2_ok"], 1)
                    if t == 1:
                        dve.wait_ge(s["exps"], j + 1)
                        dve.wait_ge(s["k2_ok"], j + 1)
                        tt(kr[:, :, 1, :], sh[:, 0, :].rearrange("p (b t) -> p b t", b=2),
                           gg[:, 0, :].rearrange("p (b t) -> p b t", b=2), ALU.mult)
                        tt(kd, k2, gg[:, 1, :], ALU.mult)
                        dve.wait_ge(s["kh_ok"], j + 1)
                        tt(kr[:, :, 0, :], kh.rearrange("p (b t) -> p b t", b=2),
                           lp.rearrange("p (b t) -> p b t", b=2), ALU.mult)
                        dve.wait_ge(s["bv_ok"], j + 1)
                        stt(bd, bv, -1.0, gg[:, 1, :], ALU.mult, ALU.mult).then_inc(s["prod_ok"], 1)
                    if t == 1:
                        shift(j, 2)
                    if t == 20:
                        shift(j, 3)
                    if t == 22:
                        dve.wait_ge(s["shifted"], j * 4 + 4)
                        dve.wait_ge(s["g_th"], j + 1)
                        stt(s2g, s2g, 1.0, sh[:, 3, :], ALU.add, ALU.mult)
                    if t == 5:
                        scores(0)
                    if t == 7:
                        scores(1)
                    if t == 17:
                        dve.wait_ge(tile_out, nt + 2)
                        stt(zp[:, 1, :], zp[:, 1, :], 1.0, zp[:, 0, :], ALU.add, ALU.mult).then_inc(s["z2_ok"], 1)
                        dve.wait_ge(s["t_in"], j * 64 + 64)
                        tt(tdt.rearrange("p (q b u) -> p q b u", q=4, b=8),
                           tc[:].unsqueeze(2).broadcast_to([P, 4, 8, BLK]),
                           m16i[:].rearrange("p (b u) -> p b u", b=8).unsqueeze(1).broadcast_to([P, 4, 8, BLK]),
                           ALU.mult).then_inc(s["tdt_ok"], 1)
                    if t == 21:
                        dve.wait_ge(s["ou_mm"], j + 1)
                        tt(xx, A, xx, ALU.add).then_inc(s["xo_ok"], 1)
                    if t == 24:
                        for b in range(2):
                            dve.wait_ge(s["nm_mm"], j * 2 + b + 1)
                            tt(nm[:, b].rearrange("p e c n -> p (e c) n"),
                               ps[:, 6 + b, :].rearrange("p (a n) -> p a n", n=64),
                               ident[:, 64:128].unsqueeze(1).broadcast_to([P, 8, 64]), ALU.add).then_inc(s["nm_ok"], 1)
                    if 25 <= t <= 31:
                        c = t - 25
                        dve.wait_ge(s["gc_ok"], j + 1)
                        dve.wait_ge(s["state_mm"], j * 7 + c + 1)
                        tt(st[64:128, :, c + 1, :], A[64:128, 0:128].rearrange("p (e n) -> p e n", e=2),
                           gcs[64:128, :, c:c + 1].broadcast_to([64, 2, 64]), ALU.mult).then_inc(s["state_ok"], 1)
                    if t == 27:
                        dve.wait_ge(s["sc_cx"], j + 1)
                        for k in range(3):
                            if k:
                                dve.wait_ge(s["sc_s"], j * 3 + k)
                                op = stt(scy, scx[:, k:k + T], col(SCW + k * CT), scy, ALU.mult, ALU.add)
                            else:
                                op = ts(scy, scx[:, 0:T], col(SCW), None, ALU.mult)
                            op.then_inc(s["sc_s"], 1)
                    if t == 29:
                        stt(scc, scc, 1.0, scb[:, 3, :], ALU.add, ALU.mult)
                        dve.wait_ge(s["sc_s"], j * 3 + 3)
                        stt(scy, scy, 0.5, scb[:, 0, :], ALU.mult, ALU.mult).then_inc(s["sc_b"], 1)
                        dve.wait_ge(s["sc_b"], j + 1)
                        tt(scf, scy, scc, ALU.mult).then_inc(s["sc_f"], 1)
                    if t == 31:
                        dve.wait_ge(s["oc_hi"], j + 1)
                        tt(olo[:, bass.ds(j, 1), :], scf.unsqueeze(1), ohi[:, bass.ds(j, 1), :].bitcast(F32),
                           ALU.subtract).then_inc(s["oc_ok"], 1)
                    if t == 9:
                        dve.wait_ge(tile_out, nt + 1)
                        conv_tap(s["x_s"], j * 4, j, 0)
                        conv_tap(s["x_s"], j * 4, j, 1)
                        stt(bon, sh[:, 0, :], col(RK), k2, ALU.mult, ALU.mult).then_inc(s["rk_ok"], 1)
                    if t == 10:
                        dve.wait_ge(s["n_in"], j * 64 + 64)
                        solve_step(1)
                        conv_tap(s["x_s"], j * 4, j, 2)
                        solve_step(2)
                        conv_tap(s["x_s"], j * 4, j, 3)
                        for k in range(3, 10):
                            solve_step(k)
                            if k == 7:
                                dve.wait_ge(s["x_th"], j + 1)
                                stt(xs2, cvt, 1.0, cv, ALU.add, ALU.mult).then_inc(s["xs_ok"], 1)
                    if t == 11:
                        for k in range(10, 13):
                            solve_step(k)
                    if t == 12:
                        dve.wait_ge(s["dat_ok"], 1)
                        dve.wait_ge(s["seg_e"], j + 1)
                        for k in range(13, 16):
                            solve_step(k)
                        seg_times(0, 0)
                        seg_times(0, 1)
                        seg_times(1, 0)
                        seg_times(1, 1).then_inc(s["seg_g"], 1)
                    if t == 16:
                        dve.wait_ge(s["rk_mm"], j + 1)
                        tt(bon, B[:, T:2 * T], sh[:, 2, :], ALU.mult).then_inc(s["bon_ok"], 1)
                    if t == 19:
                        dve.wait_ge(s["yb_mm"], j + 1)
                        stt(cv, xs2, dskh[:, bass.ds(j, 1)], C[:, 0:T], ALU.mult, ALU.add).then_inc(s["ob_d"], 1)
                        dve.wait_ge(s["ob_d"], j + 1)
                        dve.wait_ge(s["z2_ok"], j + 1)
                        stt(o[:, 1, bass.ds(j, 1), :], cv.unsqueeze(1), 0.5, zp[:, 1:2, :], ALU.mult, ALU.mult
                            ).then_inc(s["ob_ok"], 1)
                    if t == 33:
                        dve.wait_ge(s["mean_mm"], j + 1)
                        stt(yc, C[:, 0:T], -1.0 / 64, ys, ALU.mult, ALU.add).then_inc(s["yc_ok"], 1)
                    if t == 34 and not last:
                        shift_rk(j + 1)
                    if t == 36 and not last:
                        kk_floor(j + 1)
                    if t == 38 and not last:
                        kk_recip(j + 1)
                    if t == 39 and not last:
                        decays(j + 1)
                    if t == 36:
                        dve.wait_ge(s["var_rt"], j + 1)
                        v.reciprocal(rin, nrm).then_inc(s["var_r"], 1)
                        dve.wait_ge(s["var_r"], j + 1)
                        tt(yo, yc, rin, ALU.mult).then_inc(s["yn_ok"], 1)
                        dve.wait_ge(s["yn_ok"], j + 1)
                        ts(yo, yo, col(LNW), col(LNB), ALU.mult, ALU.add).then_inc(s["yl_ok"], 1)
                        dve.wait_ge(s["yl_ok"], j + 1)
                        tt(yo, yo, bon, ALU.add).then_inc(s["yb_ok"], 1)
                        dve.wait_ge(s["yb_ok"], j + 1)
                        stt(o[:, 0, bass.ds(j, 1), :], yo.unsqueeze(1), 0.5, s2g.unsqueeze(1), ALU.mult, ALU.mult
                            ).then_inc(s["oa_ok"], 1)

            with dve.Fori(0, CT - 1) as j:
                main(j, False)
            main(CT - 1, True)
            gated(0, 0, 1)

            def split_merged(k):
                r = slice(4 * k, 4 * k + 4)
                dve.wait_ge(s["m_hi"], k + 1)
                tt(hlo[:, r, :], merged[:, r, :], hhi[:, r, :].bitcast(F32), ALU.subtract).then_inc(s["m_lo"], 1)

            for n in range(3):
                if n > 0:
                    for half in range(2):
                        r = slice(4 * half, 4 * half + 4)
                        dve.wait_ge(s["osp_hi"], 2 * (n - 1) + half + 1)
                        tt(olo[:, r, :], o[:, 2 - n, r, :], ohi[:, r, :].bitcast(F32), ALU.subtract
                           ).then_inc(s["osp_lo"], 1)

                def gates(i, tail=False, group_norm=False):
                    for h in range(2):
                        for q in range(GATES):
                            y = h * GATES + q
                            gate_split(n, i, y + AHEAD)
                            if group_norm and 8 <= y:
                                g = y - 8
                                dve.wait_ge(s["gn_rt"], g + 1)
                                v.reciprocal(sqs[:, 4 + g, :], sqs[:, g, :]).then_inc(s["gn_r"], 1)
                                dve.wait_ge(s["gn_r"], g + 1)
                                for t in range(2):
                                    k = 2 * g + t
                                    stt(o[:, 1, k, :], o[:, 1, k, :], prm[:, SNW + k:SNW + k + 1], sqs[:, 4 + g, :],
                                        ALU.mult, ALU.mult).then_inc(s["gn_ok"], 1)
                        if tail and h == 1:
                            for k in range(3):
                                split_merged(k)
                        gated(n, i, h)

                if n == 0:
                    gates(1, group_norm=True)
                with dve.Fori(2 if n == 0 else 0, 3) as i:
                    gates(i)
                gates(3, tail=n == 2)
            split_lo(GATE_END + 2, 2)
            split_merged(3)
            dve.wait_ge(x_in, 48)

            def outs(i, tail):
                for h in range(2):
                    for q in range(4):
                        y = 4 * h + q + AHEAD + 1
                        if not (tail and y >= 8):
                            split_lo(GATE_END + i * 8 + y, y % RING)
                    for b in range(2):
                        if b == 0:
                            dve.wait_ge(s["out_mm"], i * 2 + (h + 1))
                        else:
                            dve.wait_ge(chunk_used, i * 8 + (GATE_END + 4 * h + 4))
                        r = xtok[:, b, bass.ds(i * (2 * CW) + h * CW, CW)]
                        tt(r, ps[:, 2 - 2 * h + b, 0:CW], r, ALU.add).then_inc(s["out_ok"], 1)
                    for b in range(2):
                        cols = bass.ds(i * (2 * CW) + h * CW, CW)
                        dve.wait_ge(s["out_ok"], i * 4 + (2 * h + b + 1))
                        tt(z[:, b, cols], xtok[:, b, cols], fnw[:, cols], ALU.mult).then_inc(s["z_ok"], 1)

            with dve.Fori(0, 3) as i:
                outs(i, False)
            outs(3, True)
            dve.wait_ge(s["f_sq"], 16)
            v.tensor_reduce(rowst[:, 0:2], rowst[:, 8:24].rearrange("p (b n) -> p b n", b=2), AX.X, ALU.add
                            ).then_inc(s["f_sum"], 1)
            dve.wait_ge(s["f_act"], 1)
            v.reciprocal(rowst[:, 4:6], rowst[:, 2:4]).then_inc(s["f_rs"], 1)
            dve.wait_ge(s["f_rs"], 1)
            dve.wait_ge(s["z_ok"], 16)
            for b, half in ((0, 0), (0, 1), (1, 0)):
                part = z[:, b, half * 1024:(half + 1) * 1024]
                ts(part, part, rowst[:, 4 + b:5 + b], None, ALU.mult).then_inc(s["f_ok"], 1)

        @block.tensor
        def _(pe):
            mm, tr = nc.tensor.matmul, nc.tensor.transpose

            pe.wait_ge(s["const_z"], 2)
            pe.wait_ge(prm_in, 13 * 16)
            tr(A[:, 0:ROWS0], prow[0:ROWS0, 0, :], ident[0:ROWS0, 0:ROWS0])
            tr(A[:, P:P + ROWS1], prow[0:ROWS1, 1, :], ident[0:ROWS1, 0:ROWS1]).then_inc(s["prm_t"], 1)
            pe.wait_ge(s["x_n"], 2)
            pe.wait_ge(s["prm_ok"], 1)

            def x_by_channel(lo, hi):
                for k in range(lo, hi):
                    if k >= 4:
                        pe.wait_ge(s["h_lo"], k - 3)
                    for b in range(2):
                        op = mm(ps[:, 4 + k % 4, b * P:(b + 1) * P], xtok[:, b, k * P:(k + 1) * P], rdiag[:, b, :],
                                start=True, stop=True)
                    op.then_inc(s["x_tr"], 1)

            def triple(dst, wcol, slot, k, khi, klo, first, last):
                a, b = whi[:, slot, k, wcol], wlo[:, slot, k, wcol]
                mm(dst, a, khi, start=first, stop=False)
                mm(dst, a, klo, start=False, stop=False)
                return mm(dst, b, khi, start=False, stop=last)

            def half_chunk(c, slot, q, t, bank, xh=hhi, xl=hlo, nq=4, width=P, done=tile_done):
                if t == 0:
                    pe.wait_ge(lo_done, c + 1)
                for k in range(KC):
                    kt = q * KC + k
                    op = triple(ps[0:width, bank + t, 0:T], slice(t * P, t * P + width), slot, k, xh[:, kt, :],
                                xl[:, kt, :], kt == 0, kt == nq * KC - 1)
                if q == nq - 1 and t == 0:
                    op.then_inc(done, 1)
                if t == 1:
                    op.then_inc(chunk_used, 1)

            x_by_channel(0, 8)
            for c in range(PRE):
                strip, q = c // 4, c % 4
                if c in (1, 2):
                    x_by_channel(4 * c + 4, 4 * c + 8)
                if c < 4:
                    pe.wait_ge(s["h_lo"], 4 * c + 4)
                for t in range(2):
                    if q == 0 and strip >= 2:
                        pe.wait_ge(tile_out, 2 * (strip - 2) + t + 1)
                    half_chunk(c, c % RING, q, t, 2 * ((strip + 1) % 2), width=16 if strip == 0 and t == 1 else P)
                if c == 22:
                    for g in range(NG):
                        pe.wait_ge(s["bc_ok"], 8)
                        bg, cg = bc[:, g, :], bc[:, NG + g, :]
                        mm(ps[:, 4 + g, 0:T], bg[:, 0:P], cg, start=True, stop=True)
                        mm(ps[:, 4 + g, T:384], bg[:, P:T], cg[:, P:T], start=True, stop=True).then_inc(s["sc_mm"], 1)
            pe.wait_ge(s["acs_ok"], 1)
            pe.wait_ge(s["scm_ok"], 4)
            for w, src in enumerate((acs[:], dts[:, 5, :])):
                for b in range(2):
                    op = tr(B[:, (2 * w + b) * 16:(2 * w + b + 1) * 16], src[:, b * P:(b + 1) * P], ident[0:16, 0:16])
            op.then_inc(s["dt_tr"], 1)
            pe.wait_ge(s["dat_ok"], 1)
            pe.wait_ge(s["lr_ok"], 1)
            pe.wait_ge(s["const_o"], 1)

            def norm_and_logits(j):
                pe.wait_ge(s["kk_sq"], j + 1)
                mm(B[:, 0:T], head1[:], ksq, start=True, stop=True).then_inc(s["kk_mm"], 1)
                pe.wait_ge(lora_in, j * 32 + 32)
                mm(A[:, 0:T], lorat[:, 0, :], lr[:], start=True, stop=True)
                mm(A[:, T:2 * T], lorat[:, 1, :], lr[:], start=True, stop=True).then_inc(s["lora_mm"], 1)

            def gate_half(n, i, y, t, first=False):
                base = MAIN_END + n * 8 * GATES
                h, q = divmod(y, GATES)
                g = 16 * n + i * 4 + 2 * h + t
                if q == 0 and first:
                    pe.wait_ge(tile_out, MAIN_TILES - 2)
                elif q == 0:
                    pe.wait_ge(tile_out, g + (MAIN_TILES - 1))
                if q == 4 and first:
                    pe.wait_ge(tile_out, MAIN_TILES)
                    pe.wait_ge(s["oc_ok"], CT)
                elif q == 4:
                    pe.wait_ge(s["gy_ok"], g - 1)
                if q == 4 and t == 0 and n > 0:
                    pe.wait_ge(s["osp_lo"], 2 * n)
                c = base + i * (2 * GATES) + y
                if q < 4:
                    half_chunk(c, (base + y) % RING, q, t, 2)
                else:
                    half_chunk(c, (base + y) % RING, q - 4, t, 0, ohi, olo, 2, done=y_done)

            norm_and_logits(0)

            def main(j, last):
                base = PRE + j * ITER
                nt = PRE_TILES + j * ITER_TILES
                free = (nt - 3, nt - 1, nt + 1, nt + 5, nt + 3)

                def score(b):
                    for e in range(2):
                        r = slice(64 * e, 64 * e + 64)
                        c = slice(b * P, b * P + P)
                        dst = ps[:, 4 + e, :]
                        krb = kr[r, b, :, :].rearrange("p w t -> p (w t)")
                        mm(dst[:, 0:T], kd[r, c], krb, start=True, stop=True)
                        mm(dst[:, T:2 * T], bd[r, c], krb, start=True, stop=True).then_inc(s["score_mm"], 1)

                for t in range(2 * (LAST + 2 * GATES) if last else SLOTS):
                    if last and t // 2 >= LAST:
                        gate_half(0, 0, t // 2 - LAST, t % 2, first=t // 2 < LAST + GATES)
                    else:
                        c, a = t // 2, t // 8
                        if t % 8 < 2:
                            pe.wait_ge(tile_out, free[a] + t % 2)
                        half_chunk(base + c, c % RING, c % 4, t % 2, BANKS[a])
                    if t == 35 and not last:
                        norm_and_logits(j + 1)
                    if t == 12:
                        pe.wait_ge(s["rk_ok"], j + 1)
                        mm(B[:, T:2 * T], head1[:], bon, start=True, stop=True).then_inc(s["rk_mm"], 1)
                    if t == 4:
                        pe.wait_ge(s["prod_ok"], j + 1)
                        for b in range(2):
                            tr(E[:, b * T:b * T + P], kd[:, b * P:(b + 1) * P], ident[:])
                            op = tr(E[:, b * T + P:b * T + T], bd[:, b * P:(b + 1) * P], ident[:])
                        op.then_inc(s["tr_kb"], 1)
                        score(0)
                        pe.wait_ge(s["shifted"], j * 4 + 3)
                        for b in range(2):
                            tr(C[:, b * T:b * T + P], sh[:, 2, b * P:(b + 1) * P], ident[:])
                            op = tr(C[:, b * T + P:b * T + T], kr[:, b, 0, :], ident[:])
                        op.then_inc(s["tr_vk"], 1)
                    if t == 6:
                        pe.wait_ge(s["score_ok"], j * 4 + 2)
                        pe.wait_ge(s["ad_ok"], j * 4 + 2)
                        score(1)
                    if t == 8:
                        pe.wait_ge(s["score_ok"], j * 4 + 4)
                        pe.wait_ge(s["kdbd_ok"], j + 1)
                        for q in range(4):
                            b, e = q // 2, q % 2
                            op = mm(E[:, q * 64:q * 64 + 64], s4[:, q, 0:P], vt[:, b, 64 * e:64 * e + 64],
                                    start=True, stop=True)
                        op.then_inc(s["xv_mm"], 1)
                    if t == 19:
                        pe.wait_ge(s["tdt_ok"], j + 1)
                        pe.wait_ge(s["xv_ok"], j + 1)
                        pe.wait_ge(s["bon_ok"], j + 1)
                        for q in range(4):
                            r = slice(q * P, q * P + P)
                            op = mm(B[:, r], tdt[:, r], xx[:, r], start=True, stop=True)
                        op.then_inc(s["u_mm"], 1)
                    if t == 20:
                        pe.wait_ge(s["u_ok"], j + 1)
                        for q in range(4):
                            r = slice(q * P, q * P + P)
                            op = mm(A[:, r], s4[:, q, 2 * P:3 * P], uu[:, r], start=True, stop=True)
                        op.then_inc(s["ou_mm"], 1)
                    if t == 21:
                        pe.wait_ge(s["xo_ok"], j + 1)
                        for q in range(4):
                            r = slice(q * P, q * P + P)
                            op = mm(B[:, r], tdt[:, r], xx[:, r], start=True, stop=True)
                        op.then_inc(s["uw_mm"], 1)
                    if t == 22:
                        pe.wait_ge(s["uw_ok"], j + 1)
                        for q in range(4):
                            b, e = q // 2, q % 2
                            r, h = slice(q * P, q * P + P), slice(64 * e, 64 * e + 64)
                            mm(A[:, r], uw[:, q, :], s4[:, q, 3 * P:4 * P], start=True, stop=False, skip_group_check=True)
                            mm(A[0:64, r], vt[:, b, h], s4[:, q, P:2 * P], start=False, stop=True, skip_group_check=True)
                            op = mm(A[64:128, r], ident[:, h], kr[:, b, 1, :], start=False, stop=True,
                                    skip_group_check=True)
                        op.then_inc(s["yz_mm"], 1)
                    if t == 23:
                        for b in range(2):
                            for e in range(2):
                                h = slice(64 * e, 64 * e + 64)
                                dst = ps[:, 6 + b, e * T:e * T + T]
                                mm(dst, uw[:, 2 * b + e, :], kdbd[:, b, 1, :, h], start=True, stop=False,
                                   skip_group_check=True)
                                op = mm(dst[0:64, :], vt[:, b, h], kdbd[:, b, 0, :, h], start=False, stop=True,
                                        skip_group_check=True)
                            op.then_inc(s["nm_mm"], 1)
                        for e in range(2):
                            op = mm(B[64:128, 8 * e:8 * e + 8], ident[:, 64 * e:64 * e + 64], gg[:, 0, 31:T:32],
                                    start=True, stop=True)
                        op.then_inc(s["gc_mm"], 1)
                    if 24 <= t <= 31:
                        c = t - 24
                        b = c // 4
                        if c == 0:
                            pe.wait_ge(s["nm_ok"], j * 2 + 2)
                            pe.wait_ge(s["yz_ok"], j + 1)
                            pe.wait_ge(s["gc_ok"], j + 1)
                        else:
                            pe.wait_ge(s["state_ok"], j * 7 + c)
                        for e in range(2):
                            if c < 7:
                                op = mm(A[64:128, 64 * e:64 * e + 64], nm[:, b, e, c % 4, :], st[:, e, c, :],
                                        start=True, stop=True)
                        if c < 7:
                            op.then_inc(s["state_mm"], 1)
                        for e in range(2):
                            u = slice(32 * (c % 4), 32 * (c % 4) + 32)
                            op = mm(B[64 * e:64 * e + 64, 32 * c:32 * c + 32], st[:, e, c, :], yz[:, 2 * b + e, u],
                                    start=True, stop=True)
                        if c == 7:
                            op.then_inc(s["y_mm"], 1)
                    if t == 9:
                        pe.wait_ge(s["acm_ok"], j + 1)
                        pe.wait_ge(s["score_ok"], j * 4 + 4)
                        pe.wait_ge(s["ad_ok"], j * 4 + 4)
                        pe.wait_ge(s["vt_ok"], j + 1)
                        mm(A, ones[0:16, :], acm[:].rearrange("p e t -> p (e t)"), start=True, stop=True
                           ).then_inc(s["acb_mm"], 1)
                    if t == 14:
                        pe.wait_ge(s["xs_ok"], j + 1)
                        for b in range(2):
                            op = tr(C[:, b * P:b * P + P], xs2[:, b * P:b * P + P], ident[:])
                        op.then_inc(s["x_tr2"], 1)
                    if t == 17:
                        pe.wait_ge(s["xst_ok"], j + 1)
                        pe.wait_ge(s["seg_g"], j + 1)
                        for e in range(2):
                            h = slice(64 * e, 64 * e + 64)
                            mm(C[h, 0:T], xst[:, 0, h], seg[:, e, 0:T], start=True, stop=False, skip_group_check=True)
                            op = mm(C[h, P:T], xst[:, 1, h], seg[:, e, T:384], start=False, stop=True,
                                    skip_group_check=True)
                        op.then_inc(s["yb_mm"], 1)
                    if t == 32:
                        pe.wait_ge(s["ys_ok"], j + 1)
                        pe.wait_ge(s["ob_d"], j + 1)
                        mm(C[:, 0:T], head1[:], ys, start=True, stop=True).then_inc(s["mean_mm"], 1)
                    if t == 34:
                        pe.wait_ge(s["ysq_ok"], j + 1)
                        mm(C[:, 0:T], head1[:], ysq, start=True, stop=True).then_inc(s["var_mm"], 1)

            with pe.Fori(0, CT - 1) as j:
                main(j, False)
            main(CT - 1, True)

            for n in range(3):
                def gates(i, group_norm=False):
                    for y in range(2 * GATES):
                        for t in range(2):
                            gate_half(n, i, y, t)
                        if group_norm and 1 <= y <= 4:
                            g = y - 1
                            pe.wait_ge(s["sq_ok"], 1)
                            mm(ps[:, 4 + g, 0:T], ones[:], sqs[:, 2 * g, :], start=True, stop=False)
                            mm(ps[:, 4 + g, 0:T], ones[:], sqs[:, 2 * g + 1, :], start=False, stop=True
                               ).then_inc(s["gn_mm"], 1)

                if n == 0:
                    gates(1, group_norm=True)
                with pe.Fori(2 if n == 0 else 0, 4) as i:
                    gates(i)

            def outs(i, peeled):
                for h in range(2):
                    for q in range(4):
                        pe.wait_ge(lo_done, GATE_END + 1 + i * 8 + (4 * h + q))
                        if peeled and h == 0:
                            pe.wait_ge(s["m_lo"], q + 1)
                        for b in range(2):
                            if q == 0:
                                if peeled:
                                    if h == 0:
                                        pe.wait_ge(tile_out, MAIN_TILES + 48)
                                    else:
                                        pe.wait_ge(s["gy_ok"], 48)
                                else:
                                    pe.wait_ge(s["out_ok"], i * 4 + (2 * h + b - 3))
                            for k in range(KC):
                                kt = q * KC + k
                                r = slice(b * P, b * P + P)
                                dst = ps[:, 2 - 2 * h + b, 0:CW]
                                mm(dst, hhi[:, kt, r], whi[:, q, k, :], start=kt == 0, stop=False)
                                mm(dst, hhi[:, kt, r], wlo[:, q, k, :], start=False, stop=False)
                                op = mm(dst, hlo[:, kt, r], whi[:, q, k, :], start=False, stop=kt == KT - 1)
                            if q == 3 and b == 0:
                                op.then_inc(s["out_mm"], 1)
                        op.then_inc(chunk_used, 1)

            outs(0, True)
            with pe.Fori(1, 4) as i:
                outs(i, False)


NAMES = ["x", "norm_w", "w_in", "rw_mu", "rw_w0", "rw_w2", "rw_a0", "rw_a2", "rw_kk", "rw_ka", "rw_rk", "rw_ln_w",
         "rw_ln_b", "ssd_conv_w", "ssd_conv_b", "ssd_dt_bias", "ssd_a_log", "ssd_d", "ssd_norm_w", "sc_conv_w",
         "w_branch", "w_out", "final_norm_w"]


def kernel(**inputs):
    import concourse.bacc as bacc
    from concourse.bass_utils import run_bass_kernel_spmd

    nc = bacc.Bacc("TRN2", target_bir_lowering=False, num_devices=1)
    arrays, args = {}, []
    for name in NAMES:
        a = np.ascontiguousarray(inputs[name])
        arrays[f"in_{name}"] = a
        args.append(nc.dram_tensor(f"in_{name}", a.shape, mybir.dt.from_np(a.dtype), kind="ExternalInput").ap())
    args.append(nc.dram_tensor("out_y", (1, T, D), F32, kind="ExternalOutput").ap())
    build_program(nc, *args)
    r = run_bass_kernel_spmd(nc, [arrays], core_ids=[0])
    return r.results[0]["out_y"]
```
